# Optimizing a Trainium2 kernel written in Bass

```python
import jax, jax.numpy as jnp
from jax import lax
import numpy as np

D_MODEL = 1024
BATCH = 1
SEQ = 256
DEPTH = 1

N_MEM = 256
ROPE_THETA = 10000.0
EPS = 1e-6
MAX_POS_OFFSET = 4096
NEG = -1e30
FORCE = 1e9

GLA_HEADS = 4
GLA_DK = D_MODEL // 2 // GLA_HEADS
GLA_DV = D_MODEL // GLA_HEADS
GLA_RANK = 16
GLA_TAU = 16.0
GLA_CHUNK = 64

NSA_HEADS = 16
NSA_KV_HEADS = 4
NSA_GROUP = NSA_HEADS // NSA_KV_HEADS
NSA_HD = D_MODEL // NSA_HEADS
CMP_LEN = 32
CMP_STRIDE = 16
CMP_HIDDEN = 256
SLC_BLOCK = 64
SLC_TOPN = 16
WINDOW = 512
NSA_Q_BLOCK = 64
N_NSA_BRANCH = 3

MEM_HEADS = 4
MEM_HD = D_MODEL // MEM_HEADS

N_BRANCH = 3
BRANCH_WIDTH = D_MODEL

SPLITS = (
    GLA_HEADS * GLA_DK,
    GLA_HEADS * GLA_DK,
    GLA_HEADS * GLA_DV,
    GLA_RANK,
    GLA_HEADS * GLA_DV,
    NSA_HEADS * NSA_HD,
    6 * NSA_KV_HEADS * NSA_HD,
    NSA_HEADS * N_NSA_BRANCH,
    NSA_HEADS * NSA_HD,
    MEM_HEADS * MEM_HD,
    MEM_HEADS * MEM_HD,
    N_BRANCH * D_MODEL,
)
D_IN = sum(SPLITS)

kernel_name = "hybrid_gla_nsa_memory_gated_block"

def rms_norm(x, gain):
    xf = x.astype(jnp.float32)
    y = xf * lax.rsqrt(jnp.mean(xf * xf, axis=-1, keepdims=True) + EPS)
    return (y * gain.astype(jnp.float32)).astype(x.dtype)

def rope(x, positions):
    half = x.shape[-1] // 2
    inv = ROPE_THETA ** (-jnp.arange(half, dtype=jnp.float32) / half)
    ang = positions.astype(jnp.float32)[..., None] * inv
    cos = jnp.cos(ang)[:, :, None, :]
    sin = jnp.sin(ang)[:, :, None, :]
    xf = x.astype(jnp.float32)
    x1, x2 = xf[..., :half], xf[..., half:]
    return jnp.concatenate([x1 * cos - x2 * sin, x2 * cos + x1 * sin], axis=-1).astype(x.dtype)

def gla_chunked(q, k, v, log_a):
    B, S, H, DK = q.shape
    DV = v.shape[-1]
    C = GLA_CHUNK
    nC = S // C
    f32 = jnp.float32

    def to_chunks(t):
        return t.astype(f32).reshape(B, nC, C, H, t.shape[-1]).transpose(1, 0, 3, 2, 4)

    qc, kc, vc = to_chunks(q), to_chunks(k), to_chunks(v)
    gc = jnp.cumsum(to_chunks(log_a), axis=3)
    causal = jnp.tril(jnp.ones((C, C), dtype=bool))

    def step(state, inp):
        qi, ki, vi, gi = inp
        diff = gi[:, :, :, None, :] - gi[:, :, None, :, :]
        decay = jnp.where(causal[:, :, None], jnp.exp(jnp.minimum(diff, 0.0)), 0.0)
        attn = jnp.einsum('bhijk,bhjk->bhij', qi[:, :, :, None, :] * decay, ki)
        o = attn @ vi + jnp.einsum('bhik,bhkv->bhiv', qi * jnp.exp(gi), state)
        g_last = gi[:, :, -1:, :]
        state = jnp.exp(g_last[:, :, 0, :])[..., None] * state + jnp.einsum(
            'bhjk,bhjv->bhkv', ki * jnp.exp(g_last - gi), vi)
        return state, o

    state0 = jnp.zeros((B, H, DK, DV), f32)
    _, o = lax.scan(step, state0, (qc, kc, vc, gc))
    return o.transpose(1, 0, 3, 2, 4).reshape(B, S, H, DV).astype(q.dtype)

def nsa_compress(tok, pe, w1, w2):
    S = tok.shape[1]
    n_cmp = (S - CMP_LEN) // CMP_STRIDE + 1
    idx = jnp.arange(n_cmp)[:, None] * CMP_STRIDE + jnp.arange(CMP_LEN)[None, :]
    blocks = tok[:, idx] + pe[None, None, :, None, :]
    h = jax.nn.gelu(jnp.einsum('bnlhd,ldf->bnhf', blocks, w1))
    return jnp.einsum('bnhf,fd->bnhd', h, w2)

def nsa_attention(q, kc, vc, k_slc, v_slc, k_win, v_win, gates):
    B, S, H, HD = q.shape
    Hkv, G, QB = NSA_KV_HEADS, NSA_GROUP, NSA_Q_BLOCK
    nQB = S // QB
    n_cmp = kc.shape[1]
    n_slc = S // SLC_BLOCK
    topn = min(SLC_TOPN, n_slc)
    scale = HD ** -0.5
    f32 = jnp.float32

    cmp_end = jnp.arange(n_cmp) * CMP_STRIDE + CMP_LEN - 1
    cs = np.arange(n_cmp)[:, None] * CMP_STRIDE
    ss = np.arange(n_slc)[None, :] * SLC_BLOCK
    ov = np.clip(np.minimum(cs + CMP_LEN, ss + SLC_BLOCK) - np.maximum(cs, ss), 0, None) / CMP_LEN
    ov = jnp.asarray(ov, f32)

    kc32, vc32 = kc.astype(f32), vc.astype(f32)
    k_sb = k_slc.reshape(B, n_slc, SLC_BLOCK, Hkv, HD).transpose(0, 3, 1, 2, 4)
    v_sb = v_slc.reshape(B, n_slc, SLC_BLOCK, Hkv, HD).transpose(0, 3, 1, 2, 4)
    kw = jnp.pad(k_win, ((0, 0), (WINDOW, 0), (0, 0), (0, 0)))
    vw = jnp.pad(v_win, ((0, 0), (WINDOW, 0), (0, 0), (0, 0)))
    qb = q.reshape(B, nQB, QB, Hkv, G, HD).transpose(1, 0, 3, 4, 2, 5)
    gb = gates.reshape(B, nQB, QB, H, N_NSA_BRANCH).transpose(1, 0, 2, 3, 4)
    bi = jnp.arange(B)[:, None, None, None]
    hi = jnp.arange(Hkv)[None, :, None, None]
    blk_id = jnp.arange(n_slc)

    def block_fn(args):
        blk, qi, gi = args
        t = blk * QB + jnp.arange(QB)
        qf = qi.astype(f32) * scale
        s = jnp.einsum('bhgqd,bnhd->bhgqn', qf, kc32)
        valid = cmp_end[None, :] <= t[:, None]
        p_cmp = jax.nn.softmax(jnp.where(valid, s, NEG), axis=-1) * valid
        o_cmp = jnp.einsum('bhgqn,bnhd->bhgqd', p_cmp, vc32)
        imp = jnp.einsum('bhgqn,ns->bhqs', p_cmp, ov)
        cur = t // SLC_BLOCK
        forced = (blk_id[None, :] == 0) | (blk_id[None, :] == cur[:, None]) | (blk_id[None, :] == cur[:, None] - 1)
        causal_blk = blk_id[None, :] <= cur[:, None]
        imp = jnp.where(forced, FORCE, jnp.where(causal_blk, imp, NEG))
        _, idx = lax.top_k(imp, topn)
        ks = k_sb[bi, hi, idx].astype(f32)
        vs = v_sb[bi, hi, idx].astype(f32)
        s = jnp.einsum('bhgqd,bhqnld->bhgqnl', qf, ks)
        kpos = idx[..., None] * SLC_BLOCK + jnp.arange(SLC_BLOCK)
        valid = kpos <= t[None, None, :, None, None]
        s = jnp.where(valid[:, :, None], s, NEG)
        p = jax.nn.softmax(s.reshape(s.shape[:4] + (-1,)), axis=-1).reshape(s.shape)
        o_slc = jnp.einsum('bhgqnl,bhqnld->bhgqd', p, vs)
        kwi = lax.dynamic_slice_in_dim(kw, blk * QB, WINDOW + QB, axis=1).astype(f32)
        vwi = lax.dynamic_slice_in_dim(vw, blk * QB, WINDOW + QB, axis=1).astype(f32)
        kp = blk * QB - WINDOW + jnp.arange(WINDOW + QB)
        valid = (kp[None, :] <= t[:, None]) & (kp[None, :] > t[:, None] - WINDOW) & (kp[None, :] >= 0)
        s = jnp.einsum('bhgqd,bkhd->bhgqk', qf, kwi)
        p = jax.nn.softmax(jnp.where(valid, s, NEG), axis=-1)
        o_win = jnp.einsum('bhgqk,bkhd->bhgqd', p, vwi)
        g = gi.astype(f32).reshape(B, QB, Hkv, G, N_NSA_BRANCH).transpose(0, 2, 3, 1, 4)
        o = g[..., 0:1] * o_cmp + g[..., 1:2] * o_slc + g[..., 2:3] * o_win
        return o.transpose(0, 3, 1, 2, 4).reshape(B, QB, H, HD).astype(q.dtype)

    out = lax.map(block_fn, (jnp.arange(nQB), qb, gb))
    return out.transpose(1, 0, 2, 3, 4).reshape(B, S, H * HD)

def memory_attention(q, k, v):
    s = jnp.einsum('bshd,bmhd->bhsm', q.astype(jnp.float32), k.astype(jnp.float32)) * (q.shape[-1] ** -0.5)
    p = jax.nn.softmax(s, axis=-1)
    return jnp.einsum('bhsm,bmhd->bshd', p, v.astype(jnp.float32)).astype(q.dtype)

def hybrid_layer(x, mem, positions, norm_gain, mem_norm_gain, w_in, w_gla_alpha, b_gla_alpha,
                 gla_out_norm, nsa_q_norm, nsa_k_norm, pe_cmp_k, pe_cmp_v, w_cmp_k1, w_cmp_k2,
                 w_cmp_v1, w_cmp_v2, w_mem_kv, mem_q_norm, mem_k_norm, w_branch, w_out):
    B, S, _ = x.shape
    xn = rms_norm(x, norm_gain)
    proj = xn @ w_in
    (gla_q, gla_k, gla_v, gla_lr, gla_gate, nsa_q, nsa_kv, nsa_g, nsa_gate,
     mem_q, mem_gate, merge) = jnp.split(proj, [int(c) for c in np.cumsum(SPLITS)[:-1]], axis=-1)

    q = gla_q.reshape(B, S, GLA_HEADS, GLA_DK) * (GLA_DK ** -0.5)
    k = gla_k.reshape(B, S, GLA_HEADS, GLA_DK)
    v = gla_v.reshape(B, S, GLA_HEADS, GLA_DV)
    log_a = jax.nn.log_sigmoid((gla_lr @ w_gla_alpha + b_gla_alpha).astype(jnp.float32)) / GLA_TAU
    o = gla_chunked(q, k, v, log_a.reshape(B, S, GLA_HEADS, GLA_DK))
    y_a = rms_norm(o, gla_out_norm).reshape(B, S, -1) * jax.nn.silu(gla_gate)

    q = rope(rms_norm(nsa_q.reshape(B, S, NSA_HEADS, NSA_HD), nsa_q_norm), positions)
    kv = nsa_kv.reshape(B, S, 6, NSA_KV_HEADS, NSA_HD)
    k_c = rope(rms_norm(kv[:, :, 0], nsa_k_norm[0]), positions)
    k_s = rope(rms_norm(kv[:, :, 2], nsa_k_norm[1]), positions)
    k_w = rope(rms_norm(kv[:, :, 4], nsa_k_norm[2]), positions)
    kc = nsa_compress(k_c, pe_cmp_k, w_cmp_k1, w_cmp_k2)
    vc = nsa_compress(kv[:, :, 1], pe_cmp_v, w_cmp_v1, w_cmp_v2)
    gates = jax.nn.sigmoid(nsa_g.reshape(B, S, NSA_HEADS, N_NSA_BRANCH))
    o = nsa_attention(q, kc, vc, k_s, kv[:, :, 3], k_w, kv[:, :, 5], gates)
    y_b = o * jax.nn.silu(nsa_gate)

    memn = rms_norm(mem, mem_norm_gain)
    mkv = (memn @ w_mem_kv).reshape(B, mem.shape[1], 2, MEM_HEADS, MEM_HD)
    mk = rms_norm(mkv[:, :, 0], mem_k_norm)
    mq = rms_norm(mem_q.reshape(B, S, MEM_HEADS, MEM_HD), mem_q_norm)
    o = memory_attention(mq, mk, mkv[:, :, 1])
    y_m = o.reshape(B, S, -1) * jax.nn.silu(mem_gate)

    branches = jnp.stack([y_a, y_b, y_m], axis=2)
    z = jnp.einsum('bscw,cwd->bscd', branches, w_branch)
    g = jax.nn.sigmoid(merge.reshape(B, S, N_BRANCH, D_MODEL))
    mixed = jnp.sum(g * z, axis=2)
    return x + mixed @ w_out

def setup_inputs(seed: int = 0) -> dict:
    key = jax.random.key(seed)
    ks = jax.random.split(key, 24)
    f32 = jnp.float32

    def normal(k, shape, scale):
        return jax.random.normal(k, shape, f32) * scale

    x = normal(ks[0], (BATCH, SEQ, D_MODEL), 1.0)
    mem = normal(ks[1], (BATCH, N_MEM, D_MODEL), 1.0)
    offset = jax.random.randint(ks[2], (BATCH,), 0, MAX_POS_OFFSET, dtype=jnp.int32)
    positions = (offset[:, None] + jnp.arange(SEQ, dtype=jnp.int32)[None, :]).astype(jnp.int32)
    return {
        "x": x,
        "mem": mem,
        "positions": positions,
        "norm_gain": 1.0 + normal(ks[3], (DEPTH, D_MODEL), 0.02),
        "mem_norm_gain": 1.0 + normal(ks[4], (DEPTH, D_MODEL), 0.02),
        "w_in": normal(ks[5], (DEPTH, D_MODEL, D_IN), D_MODEL ** -0.5),
        "w_gla_alpha": normal(ks[6], (DEPTH, GLA_RANK, GLA_HEADS * GLA_DK), GLA_RANK ** -0.5),
        "b_gla_alpha": normal(ks[7], (DEPTH, GLA_HEADS * GLA_DK), 0.1),
        "gla_out_norm": 1.0 + normal(ks[8], (DEPTH, GLA_DV), 0.02),
        "nsa_q_norm": 1.0 + normal(ks[9], (DEPTH, NSA_HD), 0.02),
        "nsa_k_norm": 1.0 + normal(ks[10], (DEPTH, N_NSA_BRANCH, NSA_HD), 0.02),
        "pe_cmp_k": normal(ks[11], (DEPTH, CMP_LEN, NSA_HD), 0.1),
        "pe_cmp_v": normal(ks[12], (DEPTH, CMP_LEN, NSA_HD), 0.1),
        "w_cmp_k1": normal(ks[13], (DEPTH, CMP_LEN, NSA_HD, CMP_HIDDEN), (CMP_LEN * NSA_HD) ** -0.5),
        "w_cmp_k2": normal(ks[14], (DEPTH, CMP_HIDDEN, NSA_HD), CMP_HIDDEN ** -0.5),
        "w_cmp_v1": normal(ks[15], (DEPTH, CMP_LEN, NSA_HD, CMP_HIDDEN), (CMP_LEN * NSA_HD) ** -0.5),
        "w_cmp_v2": normal(ks[16], (DEPTH, CMP_HIDDEN, NSA_HD), CMP_HIDDEN ** -0.5),
        "w_mem_kv": normal(ks[17], (DEPTH, D_MODEL, 2 * MEM_HEADS * MEM_HD), D_MODEL ** -0.5),
        "mem_q_norm": 1.0 + normal(ks[18], (DEPTH, MEM_HD), 0.02),
        "mem_k_norm": 1.0 + normal(ks[19], (DEPTH, MEM_HD), 0.02),
        "w_branch": normal(ks[20], (DEPTH, N_BRANCH, BRANCH_WIDTH, D_MODEL), BRANCH_WIDTH ** -0.5),
        "w_out": normal(ks[21], (DEPTH, D_MODEL, D_MODEL), D_MODEL ** -0.5),
    }

def reference(x, mem, positions, norm_gain, mem_norm_gain, w_in, w_gla_alpha, b_gla_alpha,
              gla_out_norm, nsa_q_norm, nsa_k_norm, pe_cmp_k, pe_cmp_v, w_cmp_k1, w_cmp_k2,
              w_cmp_v1, w_cmp_v2, w_mem_kv, mem_q_norm, mem_k_norm, w_branch, w_out):
    h = x
    for l in range(DEPTH):
        h = hybrid_layer(h, mem, positions, norm_gain[l], mem_norm_gain[l], w_in[l], w_gla_alpha[l],
                         b_gla_alpha[l], gla_out_norm[l], nsa_q_norm[l], nsa_k_norm[l], pe_cmp_k[l],
                         pe_cmp_v[l], w_cmp_k1[l], w_cmp_k2[l], w_cmp_v1[l], w_cmp_v2[l], w_mem_kv[l],
                         mem_q_norm[l], mem_k_norm[l], w_branch[l], w_out[l])
    return h


_drawn_inputs = setup_inputs


def setup_inputs(seed=0):
    import zlib

    import numpy as np

    out = dict(_drawn_inputs(seed))
    spreads = {}
    factors = {'norm_gain': 4.496,
     'mem_norm_gain': 8.0,
     'b_gla_alpha': 4.32,
     'gla_out_norm': 8.0,
     'nsa_q_norm': 8.0,
     'nsa_k_norm': 8.0,
     'pe_cmp_k': 8.0,
     'pe_cmp_v': 5.777,
     'w_cmp_k1': 3.054,
     'w_cmp_k2': 3.126,
     'mem_q_norm': 8.0,
     'mem_k_norm': 8.0}
    for name, (base, spread) in spreads.items():
        noise = np.random.default_rng([zlib.crc32(name.encode()), seed]).standard_normal(out[name].shape)
        drawn = base * np.exp(spread * noise) if base else spread * noise
        out[name] = __import__('jax').numpy.asarray(drawn.astype(out[name].dtype))
    for name, factor in factors.items():
        out[name] = (out[name] * factor).astype(out[name].dtype)
    return out
```

```python
from contextlib import ExitStack

import numpy as np

import concourse.bass as bass
from concourse import mybir

P = 128
SEQ, D, MEM = 256, 1024, 256
NT = SEQ // P
KB = D // P
NCOL = 512
GH, DK, DV, RANK, TAU, CHUNK = 4, 128, 256, 16, 16.0, 64
NH, NKV, HD = 16, 4, 64
HALF = HD // 2
NCMP, CSTRIDE, CLEN, CHID = 15, 16, 32, 256
NP_ = 16
MH, MHD = 4, 256
EPS, NEG = 1e-6, -1e30
SPLITS = (GH * DK, GH * DK, GH * DV, RANK, GH * DV, NH * HD, 6 * NKV * HD, NH * 3, NH * HD, MH * MHD, MH * MHD, 3 * D)
COL = [sum(SPLITS[:i]) for i in range(len(SPLITS))]
(C_GQ, C_GK, C_GV, C_LR, C_GG, C_NQ, C_NKV, C_NG, C_NGATE, C_MQ, C_MG, C_MERGE) = COL
SMALL_LR = 64
SMALL = SMALL_LR + NH * 3
TWO_PI = 2.0 * np.pi
C1 = 6.28125
C2 = float(np.float32(np.float64(TWO_PI) - C1))
C3 = float(TWO_PI - C1 - np.float64(np.float32(C2)))
MAGIC = 1.5 * 2.0 ** 23

F32, F32R, BF16 = mybir.dt.float32, mybir.dt.float32r, mybir.dt.bfloat16
U8, I32 = mybir.dt.uint8, mybir.dt.int32
ALU = mybir.AluOpType
ACT = mybir.ActivationFunctionType
AX = mybir.AxisListType.X

TABLE_SET = {ACT.Exp: "natural_log_exp_and_others", ACT.Ln: "natural_log_exp_and_others",
             ACT.Silu: "silu_and_others", ACT.Sin: "silu_and_others", ACT.Sigmoid: "sigmoid_and_others",
             ACT.Gelu_apprx_tanh: "gelu_apprx_tanh_and_others"}

JOBS = ["kv0", "kv1", "kv2", "nq0", "nq1", "small", "cmp0", "cmp1", "gq0", "gk0", "gv0", "gv1", "gg0", "gg1",
        "mgb0", "mgb1", "ng0", "ng1", "zb0", "zb1", "mga0", "mga1", "mg0", "mg1", "za0", "za1", "mq0", "mq1",
        "mk0", "mk1", "mv0", "mv1", "mgm0", "mgm1", "zm0", "zm1", "out0", "out1"]
PIECES = {j: 4 for j in JOBS}
PIECES["small"] = 1
PIECES["cmp0"] = PIECES["cmp1"] = 2
TICK_OF = {}
TICKS = []
for _j in JOBS:
    TICK_OF[_j] = len(TICKS)
    TICKS += [(_j, s) for s in range(PIECES[_j])]
NTICK = len(TICKS)
GEMMS = [j for j in JOBS]
CHAN = ("gq0", "gk0", "mq0", "mq1", "mk0", "mk1")
BRANCH = {"a": 0, "b": 1, "m": 2}
RAW_SLOTS, SPLIT_SLOTS, AHEAD = 3, 4, 2
POOL_EVERY = 3


def is_split(tick):
    return not TICKS[tick][0].startswith("cmp")


def lo_on_pool(n):
    return n % POOL_EVERY == 1 and n > 2 * POOL_EVERY


LATER = {('dve', 'o_out'): -1, ('pe', 'k_turn'): 1, ('act', 'k_turned'): 1}
URGENCY = {}


def make_plan():
    plan = {e: [[] for _ in range(NTICK + 12)] for e in ("pe", "act", "dve", "pool")}

    def at(engine, tick, step, *key):
        plan[engine][tick + LATER.get((engine, step), 0)].append((step, key))

    end = {j: TICK_OF[j] + PIECES[j] for j in JOBS}

    for b in range(3):
        T = end[f"kv{b}"]
        for t in range(NT):
            at("act", T + t, "kv_square", b, t)
            at("dve", T + t, "kv_rope", b, t)
            at("act", T + t, "kv_rstd", b, t)
            at("pool", T + t, "kv_finish", b, t)
            at("pe", T + t + 1, "k_turn", b, t)
            at("act", T + t + 1, "k_turned", b, t)
    for t in range(NT):
        at("pe", end["kv0"] + 2 + t, "vc_turn", t)
        at("act", end["kv0"] + 2 + t, "vc_turned", t)
    for kind in range(2):
        at("pool", end["kv0"] + 4 + kind, "cmp_blocks", kind)
    for i in range(2):
        T = end[f"nq{i}"]
        for t in range(NT):
            at("act", T, "q_square", i, t)
            at("dve", T, "q_rope", i, t)
            at("pool", T, "q_finish", i, t)
            at("pe", T + t + 1, "q_turn", i, t)
            at("act", T + t + 1, "q_turned", i, t)
    at("act", end["nq1"] + 2, "q_rstd")
    T = end["small"]
    at("act", T, "small_out")
    at("dve", T, "gates")
    for kind in range(2):
        T = end[f"cmp{kind}"]
        at("act", T, "cmp_gelu", kind)
        at("pe", T + 1, "cmp_turn", kind)
        at("dve", T + 1, "cmp_turned", kind)
    T = end["cmp1"] + 1
    at("pe", T + 1, "kc")
    at("dve", T + 1, "kc_out")
    at("pool", T + 1, "vc_spread")
    at("pe", T + 2, "vc")
    at("dve", T + 2, "vc_out")
    for t in range(NT):
        at("pe", T + 2 + t, "cs", t)
        at("dve", T + 2 + t, "cs_max", t)
        at("act", T + 2 + t, "cs_exp", t)
        at("dve", T + 3 + t, "cs_sum", t)
        at("pe", T + 4 + t, "cs_turn", t)
        at("dve", T + 4 + t, "cs_turned", t)
        for u in range(2):
            at("pe", T + 5 + t * 2 + u, "o", 0, t, u)
            at("dve", T + 5 + t * 2 + u, "o_out", 0, t, u)
    T = T + 6
    order = []
    for b in (1, 2):
        for t in range(NT):
            for u in range(2):
                for s in range(2 if t == 0 else 4):
                    order.append((b, t, u, s))
    for n, key in enumerate(order):
        b, t, u, s = key
        at("pe", T + n, "s", *key)
        at("dve", T + n, "s_max", *key)
        at("act", T + n, "s_exp", *key)
        at("pe", T + n + 2, "p_turn", *key)
        at("dve", T + n + 2, "p_turned", *key)
        at("pe", T + n + 3, "pv", *key)
        if s == (1 if t == 0 else 3):
            at("dve", T + n + 4, "o_out", b, t, u)
    nsa_end = T + len(order) + 4
    for lv in range(7):
        at("pool", end["gq0"] + 2 * lv, "level_mask", lv)
    for job in ("gq0", "gk0"):
        at("act", end[job], "gqk_out", job)
    for i in range(2):
        for t in range(NT):
            at("dve", end[f"gv{i}"] + t, "gv_out", i, t)
            at("act", end[f"gg{i}"] + t // 2, "silu", f"gg{i}", t)
            at("pool", end[f"gg{i}"] + 1 + t, "gla_gain", i, t)
    T = end["gg0"]
    for z in range(2):
        at("pe", T + 1 + z, "z", z)
        at("act", T + 1 + z, "z_abs", z)
        at("dve", T + 1 + z, "z_min", z)
    at("act", T + 3, "z_log")
    at("dve", T + 3, "cumsum")
    T = max(nsa_end, end["gg1"]) + 1
    at("act", T, "chunk_exp_q")
    at("dve", T, "chunk_k")
    at("act", T, "chunk_exp_k")
    at("dve", T + 1, "chunk_mult")
    levels = ["diag", "chunk", 0, 1, 2, 3, 4, 5, "tiles"]
    T = T + 2
    for n, lv in enumerate(levels):
        L = T + 2 * n
        if lv not in ("diag", "chunk"):
            at("dve", L - 2, "level_diff", lv)
            if lv != "tiles":
                at("act", L - 2, "level_exp", lv)
                at("dve", L - 1, "level_k", lv)
                at("pool", L - 1, "level_q", lv)
        for t in range(NT if lv != "tiles" else 1):
            at("pe", L + t, "level", lv, t)
            at("dve", L + t, "level_take", lv, t)
    T = T + 2 * len(levels)
    for n in range(4):
        at("pe", T + n, "go", n // 2, n % 2)
        at("act", T + n, "go_rstd", n // 2, n % 2)
        at("dve", T + n, "go_out", n // 2, n % 2)
    gla_end = T + 4
    for i in range(2):
        for t in range(NT):
            at("act", end[f"ng{i}"], "silu", f"ng{i}", t)
            at("dve", end[f"ng{i}"], "nsa_gate", i, t)
    for c in ("b", "a", "m"):
        for i in range(2):
            for t in range(NT):
                T = {"b": end[f"ng{i}"] + t, "a": gla_end + 1 + 2 * i + t, "m": end["mv1"] + 5 + 2 * i + t}[c]
                at("pe", T, "y_turn", c, i, t)
                at("act", T, "y_hi", c, i, t)
                at("dve", T, "y_lo", c, i, t)
                at("act", end[f"mg{c}{i}"], "merge", c, i, t)
                at("dve", end[f"z{c}{i}"] + t // 2, "mix", c, i, t)
                if c != "b":
                    at("pool" if c != "m" else "dve", end[f"z{c}{i}"] + t // 2, "mix_add", c, i, t)
    T = end["mg1"] + 4
    for t in range(NT):
        at("act", T, "mem_square", t)
    at("act", T, "mem_rstd")
    for t in range(NT):
        at("dve", T + 1, "mem_norm", t)
    T = end["za1"] - 2
    for g in range(4):
        at("pe", T + 3 + g, "mt_turn", g)
        at("act", T + 3 + g, "mt_hi", g)
        at("dve", T + 3 + g, "mt_lo", g)
    for i in range(2):
        at("act", end[f"mq{i}"], "mq_square", i)
        at("dve", end[f"mq{i}"], "mq_out", i)
        at("pe", end[f"mq{i}"] + 1, "mq_sum", i)
        at("act", end[f"mq{i}"] + 1, "mq_rstd", i)
        for t in range(NT):
            at("act", end[f"mg{i}"], "silu", f"mg{i}", t)
        at("act", end[f"mk{i}"], "mk_square", i)
        at("dve", end[f"mk{i}"], "mk_out", i)
        at("pe", end[f"mk{i}"] + 1, "mk_sum", i)
        at("act", end[f"mk{i}"] + 1, "mk_rstd", i)
        at("dve", end[f"mk{i}"] + 2, "mk_norm", i)
        for t in range(NT):
            at("dve", end[f"mv{i}"] + t, "mv_out", i, t)
    T = end["mv1"]
    for n in range(4):
        key = (n % 2, n // 2)
        at("pe", T + n, "ms", *key)
        at("dve", T + n, "ms_max", *key)
        at("act", T + n, "ms_exp", *key)
        at("pe", T + n + 1, "mp_turn", *key)
        at("dve", T + n + 1, "mp_turned", *key)
        at("pe", T + n + 2, "mo", *key)
        at("dve", T + n + 2, "mo_out", *key)
    for i in range(2):
        for t in range(NT):
            at("pe", end[f"z{'m'}{i}"] + (t // 2), "y_turn", "out", i, t)
            at("act", end[f"z{'m'}{i}"] + (t // 2), "y_hi", "out", i, t)
            at("dve", end[f"z{'m'}{i}"] + (t // 2), "y_lo", "out", i, t)
    for i in range(2):
        for t in range(NT):
            at("dve", end[f"out{i}"], "final", i, t)
    return {e: [sorted(tick, key=lambda item: URGENCY.get((e, item[0]), 0)) for tick in ticks]
            for e, ticks in plan.items()}


PLAN = make_plan()


def keys_of(engine, step):
    return [key for tick in PLAN[engine] for s, key in tick if s == step]


class Signal:

    def __init__(self, sem, keys, per=1):
        self.sem, self.per = sem, per
        self.place = {k: n for n, k in enumerate(keys)}

    def of(self, *key, part=None):
        return self.place[key] * self.per + (self.per if part is None else part + 1)


class Count:

    def __init__(self):
        self.value = 0

    def next(self):
        self.value += 1
        return self.value


def unit_heads(t, q):
    return range(q, 8, 2) if t == 0 else range(4 * (q // 2) + q % 2, 4 * (q // 2) + 4, 2)


RING_BANKS = (4, 5, 6)
OUT_BANK = 7
RING_STEPS = ("vec_turn", "xt_turn", "k_turn", "vc_turn", "q_turn", "cmp_turn", "kc", "vc", "cs",
              "cs_turn", "s", "p_turn", "z", "level", "go", "y_turn", "mt_turn", "mq_sum",
              "mk_sum", "ms", "mp_turn", "mo")


def ring_plan():
    uses = [("vec_turn", ())] + [("xt_turn", (g,)) for g in range(4)]
    uses += [(s, k) for tick in PLAN["pe"] for s, k in tick if s in RING_STEPS]
    bank = {use: RING_BANKS[n % len(RING_BANKS)] for n, use in enumerate(uses)}
    before = {use: uses[n - len(RING_BANKS)] if n >= len(RING_BANKS) else None for n, use in enumerate(uses)}
    return bank, before


def layer(nc, x, mem, positions, norm_gain, mem_norm_gain, w_in, w_gla_alpha, b_gla_alpha, gla_out_norm,
          nsa_q_norm, nsa_k_norm, pe_cmp_k, pe_cmp_v, w_cmp_k1, w_cmp_k2, w_cmp_v1, w_cmp_v2, w_mem_kv,
          mem_q_norm, mem_k_norm, w_branch, w_out, rope_inv, out):
    ring_bank, ring_before = ring_plan()
    ctx = ExitStack()
    with ctx:
        def sb(name, shape, dt=F32):
            return ctx.enter_context(nc.sbuf_tensor(name, shape, dt))

        def sem(name):
            return ctx.enter_context(nc.semaphore(name))

        raw = sb("raw", [P, RAW_SLOTS, 4, NCOL])
        whi = sb("whi", [P, SPLIT_SLOTS, 2 * NCOL], F32R)
        wlo = sb("wlo", [P, SPLIT_SLOTS, 2 * NCOL], F32R)
        xth = sb("xth", [P, KB, SEQ], F32R)
        xtl = sb("xtl", [P, KB, SEQ], F32R)
        yth = sb("yth", [P, KB, SEQ], F32R)
        ytl = sb("ytl", [P, KB, SEQ], F32R)
        xtok = sb("xtok", [P, NT, D])
        ob = sb("ob", [P, NT, D])
        oa = sb("oa", [P, NT, D])
        acc = sb("acc", [P, NT, D])
        qtok = acc
        s1 = sb("s1", [P, 2048])
        s2 = sb("s2", [P, 2048])
        s3 = sb("s3", [P, 2048])
        s4 = sb("s4", [P, 2048])
        s5 = sb("s5", [P, 2048])
        s6 = sb("s6", [P, 2048])
        s7 = sb("s7", [P, 2048])
        s8 = sb("s8", [P, 2048])
        qt = s1[:, :].rearrange("p (j s) -> p j s", j=8)
        kt = s2[:, :].rearrange("p (b g s) -> p b g s", b=2, g=NKV)
        ct = s3[:, :].rearrange("p (b g s) -> p b g s", b=2, g=NKV)
        probs = s3[:, 0:1024].rearrange("p (b n) -> p b n", b=2)
        probs_t = s3[:, 1024:2048].rearrange("p (b n) -> p b n", b=2)
        blocks = oa[:, :, 0:960].rearrange("p k (c n) -> p k c n", c=16)
        vs = sb("vs", [P, 2, NT, NKV * HD])
        qg = s4[:, 0:1024].rearrange("p (h s) -> p h s", h=GH)
        kg = s4[:, 1024:2048].rearrange("p (h s) -> p h s", h=GH)
        vg = s5[:, :].rearrange("p (t n) -> p t n", t=NT)
        lvk = [s6[:, 0:1024], s1[:, 0:1024]]
        lvq = [s6[:, 1024:2048], s1[:, 1024:2048]]
        gsum = s7[:, 0:1024]
        gexp = s7[:, 1024:2048]
        kh = s2[:, 0:1024].rearrange("p (h s) -> p h s", h=GH)
        qh = s2[:, 1024:2048].rearrange("p (h s) -> p h s", h=GH)
        att = s3[:, 0:1024].rearrange("p (t h i) -> p t h i", t=NT, h=GH)
        att10 = s3[:, 1024:1536].rearrange("p (h i) -> p h i", h=GH)
        mkt = s1[:, :].rearrange("p (h c s) -> p h c s", h=MH, c=2)
        mqt = s4[:, :].rearrange("p (h c s) -> p h c s", h=MH, c=2)
        mv = s5[:, :].rearrange("p (t n) -> p t n", t=NT)
        memx = s7[:, :].rearrange("p (t n) -> p t n", t=NT)
        msq = s6[:, :].rearrange("p (b n) -> p b n", b=4)
        mprobs = s3[:, 0:1024].rearrange("p (b n) -> p b n", b=2)
        mprobs_t = s3[:, 1024:2048].rearrange("p (b n) -> p b n", b=2)
        rope_a = s8[:, 0:512]
        rope_b = s8[:, 512:1024]
        kdup = s8[:, 1024:1536]
        vdup = s6[:, 0:1024].rearrange("p (t n) -> p t n", t=NT)
        squares = s8[:, 1536:2048]
        mgate = s8[:, :].rearrange("p (i t n) -> p i t n", i=2, t=NT)
        zgate = sb("zgate", [P, NT, NCOL])
        oprod = zgate[:, 0, :]
        mixed = s2[:, 0:1024].rearrange("p (t n) -> p t n", t=NT)
        ident = sb("ident", [P, P])
        ident_b = sb("ident_b", [P, P], BF16)
        causal = sb("causal", [P, P], BF16)
        cmask = sb("cmask", [P, NT, NP_], BF16)
        cvalid = sb("cvalid", [P, NT, NP_])
        headsel = sb("headsel", [P, 8])
        lmask = sb("lmask", [P, 7, P], U8)
        lmask_f = sb("lmask_f", [P, P])
        ones = sb("ones", [P, P])
        eps = sb("eps", [P, 1])
        half_pi = sb("half_pi", [P, 1])
        ln_scale = sb("ln_scale", [P, 2])
        vec = sb("vec", [56, P])
        vect = sb("vect", [P, 56])
        gain, mgain, balpha = vect[:, 0:8], vect[:, 8:16], vect[:, 16:20]
        mqk_gain = sb("mqk_gain", [P, 2])
        gla_norm = sb("gla_norm", [P, DV])
        qk_norm = sb("qk_norm", [P, 4, HD])
        inv = sb("inv", [P, HALF])
        pos_i = sb("pos_i", [P, NT], I32)
        rope_c = s5[:, 0:512].rearrange("p (v t a d) -> p v t a d", v=4, t=NT, a=2)
        rope_s = s5[:, 512:1024].rearrange("p (v t a d) -> p v t a d", v=4, t=NT, a=2)
        ang = s5[:, 1024:1280].rearrange("p (v t d) -> p v t d", v=4, t=NT)
        cosines = s5[:, 1280:1344].rearrange("p (t d) -> p t d", t=NT)
        sines = s5[:, 1344:1408].rearrange("p (t d) -> p t d", t=NT)
        walpha = sb("walpha", [RANK, GH * DK])
        w2 = sb("w2", [P, 2, 2, 2, HD])
        lrt = sb("lrt", [RANK, SEQ])
        gates = sb("gates", [P, NT, NH * 3])
        ssx = sb("ssx", [P, 4])
        rsx = sb("rsx", [P, 4])
        ssk = sb("ssk", [P, 3, NT, NKV])
        rsk = sb("rsk", [P, 3, NT, NKV])
        ssq = sb("ssq", [P, NT, NH])
        rsq = sb("rsq", [P, NT, NH])
        hid = s6[0:60, 1024:1536].rearrange("p (k f) -> p k f", k=2)
        hid_t = sb("hid_t", [P, 2, 2, 60])
        kcc = sb("kcc", [P, NKV, 2, NP_])
        hrep = s6[:, 1536:2048].rearrange("p (f u g h n) -> p f u g h n", f=2, u=2, g=2, h=4)
        vbd = s7[:, 0:1024].rearrange("p (u h d) -> p u h d", u=2, h=8)
        csc = s7[:, 1536:2048].rearrange("p (t h n) -> p t h n", t=NT, h=NH)
        csm = sb("csm", [P, NT, NH])
        cpt = s7[:, 1024:1536].rearrange("p (t u q) -> p t u q", t=NT, u=2)
        smax = sb("smax", [P, 4, 4])
        nbias = sb("nbias", [P, 4, 4])
        ssum = sb("ssum", [P, 3, NT, NH])
        oweight = sb("oweight", [P, 8])
        glast = sb("glast", [P, GH, 4])
        sso = sb("sso", [P, NT, GH])
        rso = sb("rso", [P, NT, GH])
        rsmq = sb("rsmq", [P, MH, NT])
        msum = sb("msum", [P, NT, MH])
        ps = ctx.enter_context(nc.psum_tensor("ps", [P, 8, 512], F32))

        x_in = [sem(f"x_in{t}") for t in range(NT)]
        vec_in, small_in, mem_in = sem("vec_in"), sem("small_in"), sem("mem_in")
        raw_in = [sem(f"raw_in{i}") for i in range(RAW_SLOTS)]
        small_w = sem("small_w")
        out_written = sem("out_written")
        consts = sem("consts")
        act_chain, dve_chain, pool_chain = sem("act_chain"), sem("dve_chain"), sem("pool_chain")
        splits = [n for n in range(NTICK) if is_split(n)]
        order_of = {tick: n for n, tick in enumerate(splits)}
        hi_made = Signal(sem("hi_made"), [(n,) for n in range(len(splits))])
        lo_made_dve = Signal(sem("lo_made_dve"), [(n,) for n in range(len(splits)) if not lo_on_pool(n)])
        lo_made_pool = Signal(sem("lo_made_pool"), [(n,) for n in range(len(splits)) if lo_on_pool(n)])
        piece_done = Signal(sem("piece_done"), [(n,) for n in range(NTICK)])

        def lo_made(n):
            return lo_made_pool if lo_on_pool(n) else lo_made_dve

        out_units = [k[:3] for tick in PLAN["pe"] for s, k in tick if s == "o" or (s == "pv" and k[3] == 0)]
        k_turn_done = Signal(sem("k_turn_done"), keys_of("pe", "k_turn"))
        vc_turn_done = Signal(sem("vc_turn_done"), keys_of("pe", "vc_turn"))
        q_turn_done = Signal(sem("q_turn_done"), keys_of("pe", "q_turn"))
        cmp_turn_done = Signal(sem("cmp_turn_done"), keys_of("pe", "cmp_turn"))
        kc_done = Signal(sem("kc_done"), keys_of("pe", "kc"))
        vc_done = Signal(sem("vc_done"), keys_of("pe", "vc"))
        cs_done = Signal(sem("cs_done"), keys_of("pe", "cs"))
        cs_turn_done = Signal(sem("cs_turn_done"), keys_of("pe", "cs_turn"))
        o_done = Signal(sem("o_done"), keys_of("pe", "o"))
        s_done = Signal(sem("s_done"), keys_of("pe", "s"))
        p_turn_done = Signal(sem("p_turn_done"), keys_of("pe", "p_turn"))
        pv_done = Signal(sem("pv_done"), keys_of("pe", "pv"))
        z_done = Signal(sem("z_done"), keys_of("pe", "z"))
        level_done = Signal(sem("level_done"), keys_of("pe", "level"))
        go_done = Signal(sem("go_done"), keys_of("pe", "go"))
        y_turn_done = Signal(sem("y_turn_done"), keys_of("pe", "y_turn"))
        mt_turn_done = Signal(sem("mt_turn_done"), keys_of("pe", "mt_turn"))
        mq_sum_done = Signal(sem("mq_sum_done"), keys_of("pe", "mq_sum"))
        mk_sum_done = Signal(sem("mk_sum_done"), keys_of("pe", "mk_sum"))
        ms_done = Signal(sem("ms_done"), keys_of("pe", "ms"))
        mp_turn_done = Signal(sem("mp_turn_done"), keys_of("pe", "mp_turn"))
        mo_done = Signal(sem("mo_done"), keys_of("pe", "mo"))
        kv_square_done = Signal(sem("kv_square_done"), keys_of("act", "kv_square"))
        kv_rstd_done = Signal(sem("kv_rstd_done"), keys_of("act", "kv_rstd"))
        k_turned_done = Signal(sem("k_turned_done"), keys_of("act", "k_turned"))
        vc_turned_done = Signal(sem("vc_turned_done"), keys_of("act", "vc_turned"))
        q_square_done = Signal(sem("q_square_done"), keys_of("act", "q_square"))
        q_turned_done = Signal(sem("q_turned_done"), keys_of("act", "q_turned"))
        q_rstd_done = Signal(sem("q_rstd_done"), keys_of("act", "q_rstd"))
        small_out_done = Signal(sem("small_out_done"), keys_of("act", "small_out"))
        cmp_gelu_done = Signal(sem("cmp_gelu_done"), keys_of("act", "cmp_gelu"))
        cs_exp_done = Signal(sem("cs_exp_done"), keys_of("act", "cs_exp"))
        s_exp_done = Signal(sem("s_exp_done"), keys_of("act", "s_exp"))
        gqk_out_done = Signal(sem("gqk_out_done"), keys_of("act", "gqk_out"))
        z_abs_done = Signal(sem("z_abs_done"), keys_of("act", "z_abs"))
        z_log_done = Signal(sem("z_log_done"), keys_of("act", "z_log"))
        chunk_exp_q_done = Signal(sem("chunk_exp_q_done"), keys_of("act", "chunk_exp_q"))
        chunk_exp_k_done = Signal(sem("chunk_exp_k_done"), keys_of("act", "chunk_exp_k"))
        level_exp_done = Signal(sem("level_exp_done"), keys_of("act", "level_exp"))
        go_rstd_done = Signal(sem("go_rstd_done"), keys_of("act", "go_rstd"))
        silu_done = Signal(sem("silu_done"), keys_of("act", "silu"))
        y_hi_done = Signal(sem("y_hi_done"), keys_of("act", "y_hi"))
        merge_done = Signal(sem("merge_done"), keys_of("act", "merge"))
        mem_square_done = Signal(sem("mem_square_done"), keys_of("act", "mem_square"))
        mem_rstd_done = Signal(sem("mem_rstd_done"), keys_of("act", "mem_rstd"))
        mt_hi_done = Signal(sem("mt_hi_done"), keys_of("act", "mt_hi"))
        mq_square_done = Signal(sem("mq_square_done"), keys_of("act", "mq_square"))
        mq_rstd_done = Signal(sem("mq_rstd_done"), keys_of("act", "mq_rstd"))
        mk_square_done = Signal(sem("mk_square_done"), keys_of("act", "mk_square"))
        mk_rstd_done = Signal(sem("mk_rstd_done"), keys_of("act", "mk_rstd"))
        ms_exp_done = Signal(sem("ms_exp_done"), keys_of("act", "ms_exp"))
        kv_rope_done = Signal(sem("kv_rope_done"), keys_of("dve", "kv_rope"))
        q_rope_done = Signal(sem("q_rope_done"), keys_of("dve", "q_rope"))
        gates_done = Signal(sem("gates_done"), keys_of("dve", "gates"))
        cmp_turned_done = Signal(sem("cmp_turned_done"), keys_of("dve", "cmp_turned"))
        kc_out_done = Signal(sem("kc_out_done"), keys_of("dve", "kc_out"))
        vc_out_done = Signal(sem("vc_out_done"), keys_of("dve", "vc_out"))
        cs_max_done = Signal(sem("cs_max_done"), keys_of("dve", "cs_max"))
        cs_sum_done = Signal(sem("cs_sum_done"), keys_of("dve", "cs_sum"))
        cs_turned_done = Signal(sem("cs_turned_done"), keys_of("dve", "cs_turned"))
        s_max_done = Signal(sem("s_max_done"), keys_of("dve", "s_max"))
        p_turned_done = Signal(sem("p_turned_done"), keys_of("dve", "p_turned"))
        o_out_done = Signal(sem("o_out_done"), keys_of("dve", "o_out"))
        gv_out_done = Signal(sem("gv_out_done"), keys_of("dve", "gv_out"))
        z_min_done = Signal(sem("z_min_done"), keys_of("dve", "z_min"))
        cumsum_done = Signal(sem("cumsum_done"), keys_of("dve", "cumsum"))
        chunk_k_done = Signal(sem("chunk_k_done"), keys_of("dve", "chunk_k"))
        chunk_mult_done = Signal(sem("chunk_mult_done"), keys_of("dve", "chunk_mult"))
        level_diff_done = Signal(sem("level_diff_done"), keys_of("dve", "level_diff"))
        level_k_done = Signal(sem("level_k_done"), keys_of("dve", "level_k"))
        level_take_done = Signal(sem("level_take_done"), keys_of("dve", "level_take"))
        go_out_done = Signal(sem("go_out_done"), keys_of("dve", "go_out"))
        nsa_gate_done = Signal(sem("nsa_gate_done"), keys_of("dve", "nsa_gate"))
        y_lo_done = Signal(sem("y_lo_done"), keys_of("dve", "y_lo"))
        mix_done = Signal(sem("mix_done"), keys_of("dve", "mix"))
        mem_norm_done = Signal(sem("mem_norm_done"), keys_of("dve", "mem_norm"))
        mt_lo_done = Signal(sem("mt_lo_done"), keys_of("dve", "mt_lo"))
        mq_out_done = Signal(sem("mq_out_done"), keys_of("dve", "mq_out"))
        mk_out_done = Signal(sem("mk_out_done"), keys_of("dve", "mk_out"))
        mk_norm_done = Signal(sem("mk_norm_done"), keys_of("dve", "mk_norm"))
        mv_out_done = Signal(sem("mv_out_done"), keys_of("dve", "mv_out"))
        ms_max_done = Signal(sem("ms_max_done"), keys_of("dve", "ms_max"))
        mp_turned_done = Signal(sem("mp_turned_done"), keys_of("dve", "mp_turned"))
        mo_out_done = Signal(sem("mo_out_done"), keys_of("dve", "mo_out"))
        final_done = Signal(sem("final_done"), keys_of("dve", "final"))
        kv_finish_done = Signal(sem("kv_finish_done"), keys_of("pool", "kv_finish"))
        q_finish_done = Signal(sem("q_finish_done"), keys_of("pool", "q_finish"))
        cmp_blocks_done = Signal(sem("cmp_blocks_done"), keys_of("pool", "cmp_blocks"), per=4)
        vc_spread_done = Signal(sem("vc_spread_done"), keys_of("pool", "vc_spread"), per=4)
        gla_gain_done = Signal(sem("gla_gain_done"), keys_of("pool", "gla_gain"))
        level_q_done = Signal(sem("level_q_done"), keys_of("pool", "level_q"))
        vec_turn_done = Signal(sem("vec_turn_done"), [()])
        xt_turn_done = Signal(sem("xt_turn_done"), [(g,) for g in range(4)])
        xt_hi_done = Signal(sem("xt_hi_done"), [(g,) for g in range(4)])
        x_rstd_done = Signal(sem("x_rstd_done"), [()])
        sincos_done = Signal(sem("sincos_done"), [()])
        kv_sum_done = Signal(sem("kv_sum_done"), keys_of("dve", "kv_rope"))
        q_sum_done = Signal(sem("q_sum_done"), keys_of("dve", "q_rope"))
        x_norm_done = Signal(sem("x_norm_done"), [(0,), (1,)])
        xt_lo_done = Signal(sem("xt_lo_done"), [(g,) for g in range(4)])
        vec_turned_done = Signal(sem("vec_turned_done"), [()])
        angles_done = Signal(sem("angles_done"), [()])
        rope_tables_done = Signal(sem("rope_tables_done"), [()])
        mix_add_pool = Signal(sem("mix_add_pool"), keys_of("pool", "mix_add"))
        mix_add_dve = Signal(sem("mix_add_dve"), keys_of("dve", "mix_add"))
        ring_readers = {
            "vec_turn": vec_turned_done,
            "xt_turn": xt_lo_done,
            "k_turn": k_turned_done,
            "vc_turn": vc_turned_done,
            "q_turn": q_turned_done,
            "cmp_turn": cmp_turned_done,
            "kc": kc_out_done,
            "vc": vc_out_done,
            "cs": cs_max_done,
            "cs_turn": cs_turned_done,
            "s": s_exp_done,
            "p_turn": p_turned_done,
            "z": z_min_done,
            "level": level_take_done,
            "go": go_out_done,
            "y_turn": y_lo_done,
            "mt_turn": mt_lo_done,
            "mq_sum": mq_rstd_done,
            "mk_sum": mk_rstd_done,
            "ms": ms_exp_done,
            "mp_turn": mp_turned_done,
            "mo": mo_out_done,
        }

        def ring(name, *key):
            return ps[:, ring_bank[(name, key)], :]

        def ring_reader(name, *key):
            return ring_readers[ring_before[(name, key)][0]].sem

        def ring_read(name, *key):
            before, its_key = ring_before[(name, key)]
            return ring_readers[before].of(*its_key)

        def job_end(job):
            return piece_done.of(TICK_OF[job] + PIECES[job] - 1)

        def job_bank(job, t):
            return ps[:, (JOBS.index(job) % 2) * 2 + t, :]

        def job_readers(job):
            if job.startswith("kv"):
                return [(kv_rope_done, (int(job[2]), t)) for t in range(NT)]
            if job.startswith("nq"):
                return [(q_rope_done, (int(job[2]), t)) for t in range(NT)]
            if job == "small":
                return [(small_out_done, ())]
            if job.startswith("cmp"):
                return [(cmp_gelu_done, (int(job[3]),))]
            if job in ("gq0", "gk0"):
                return [(gqk_out_done, (job,))]
            if job.startswith("gv"):
                return [(gv_out_done, (int(job[2]), t)) for t in range(NT)]
            if job[:2] in ("gg", "ng") or job in ("mg0", "mg1"):
                return [(silu_done, (job, t)) for t in range(NT)]
            if job.startswith("mq"):
                return [(mq_out_done, (int(job[2]),))]
            if job.startswith("mk"):
                return [(mk_out_done, (int(job[2]),))]
            if job.startswith("mv"):
                return [(mv_out_done, (int(job[2]), t)) for t in range(NT)]
            if job.startswith("mg"):
                return [(merge_done, (job[2], int(job[3]), t)) for t in range(NT)]
            if job.startswith("z"):
                return [(mix_done, (job[1], int(job[2]), t)) for t in range(NT)]
            return [(final_done, (int(job[3]), t)) for t in range(NT)]

        loads = []
        for j in JOBS:
            if j == "small":
                loads.append((j, 0, 1))
            elif j.startswith("cmp"):
                loads += [(j, 0, 1), (j, 1, 1)]
            else:
                loads += [(j, 0, 2), (j, 2, 2)]
        load_of = {TICK_OF[j] + s0 + d: n for n, (j, s0, k) in enumerate(loads) for d in range(k)}

        def raw_piece(tick):
            job, s = TICKS[tick]
            slot = load_of[tick] % RAW_SLOTS
            if job == "small":
                return raw[:, slot, 0:2, :].rearrange("p k n -> p (k n)")[:, 0:KB * SMALL]
            return raw[:, slot, 2 * (s % 2):2 * (s % 2) + 2, :].rearrange("p k n -> p (k n)")

        def split_width(tick):
            return KB * SMALL if TICKS[tick][0] == "small" else 2 * NCOL

        def raw_sem(tick):
            return raw_in[load_of[tick] % RAW_SLOTS]

        def raw_value(tick):
            return (load_of[tick] // RAW_SLOTS + 1) * 16

        block = ctx.enter_context(nc.Block())

        @block.sync
        def _(sp):
            for t in range(NT):
                sp.dma_start(xtok[:, t, :], x[0, t * P:(t + 1) * P, :]).then_inc(x_in[t], 16)

            def weights(n):
                job, s0, k = loads[n]
                slot = n % RAW_SLOTS
                if n >= RAW_SLOTS:
                    j0, p0, k0 = loads[n - RAW_SLOTS]
                    for tick in range(TICK_OF[j0] + p0, TICK_OF[j0] + p0 + k0):
                        if is_split(tick):
                            m = order_of[tick]
                            sp.wait_ge(hi_made.sem, hi_made.of(m))
                            sp.wait_ge(lo_made(m).sem, lo_made(m).of(m))
                        else:
                            sp.wait_ge(piece_done.sem, piece_done.of(tick))
                if job == "small":
                    dst = raw[:, slot, 0:2, :].rearrange("p k n -> p (k n)")[:, 0:KB * SMALL]
                    dst = dst.rearrange("p (k n) -> p k n", k=KB)
                    src = w_in[0].rearrange("(k p) n -> p k n", p=P)
                    sp.dma_start(dst[:, :, 0:SMALL_LR], src[:, :, C_LR:C_LR + SMALL_LR]).then_inc(small_w, 16)
                    sp.dma_start(dst[:, :, SMALL_LR:], src[:, :, C_NG:C_NG + NH * 3]).then_inc(raw_in[slot], 16)
                    return
                if job.startswith("cmp"):
                    w1 = (w_cmp_k1, w_cmp_v1)[int(job[3])]
                    src = w1[0].rearrange("(c l) d f -> (l d) c f", l=2)[:, 8 * s0:8 * s0 + 8, :]
                    dst = raw[:, slot, :, :].rearrange("p a n -> p (a n)").rearrange("p (c f) -> p c f", c=8)
                    sp.dma_start(dst, src).then_inc(raw_in[slot], 16)
                    return
                if job.startswith("mk") or job.startswith("mv"):
                    w, c0 = w_mem_kv[0], (D if job[1] == "v" else 0) + int(job[2]) * NCOL
                elif job[0] == "z":
                    w, c0 = w_branch[0, BRANCH[job[1]]], int(job[2]) * NCOL
                elif job.startswith("out"):
                    w, c0 = w_out[0], int(job[3]) * NCOL
                elif job.startswith("mg") and job[2] in BRANCH:
                    w, c0 = w_in[0], C_MERGE + BRANCH[job[2]] * D + int(job[3]) * NCOL
                else:
                    c0 = {"kv": C_NKV, "nq": C_NQ, "gq": C_GQ, "gk": C_GK, "gv": C_GV, "gg": C_GG, "ng": C_NGATE,
                          "mq": C_MQ, "mg": C_MG}[job[:2]] + int(job[2]) * NCOL
                    w = w_in[0]
                src = w.rearrange("(k p) n -> p k n", p=P)[:, 2 * s0:2 * s0 + 4, c0:c0 + NCOL]
                sp.dma_start(raw[:, slot, :, :], src).then_inc(raw_in[slot], 16)

            row = 0
            for v in (norm_gain, mem_norm_gain, b_gla_alpha, mem_q_norm, mem_k_norm):
                n = v.shape[1] // P
                sp.dma_start(vec[row:row + n, :], v[0].rearrange("(c p) -> c p", p=P)).then_inc(vec_in, 16)
                row += n
            for v in (pe_cmp_k, pe_cmp_v):
                sp.dma_start(vec[row:row + 16, :], v[0].rearrange("(c l) d -> c (l d)", l=2)).then_inc(vec_in, 16)
                row += 16
            weights(0)
            sp.dma_start(pos_i[:, :], positions[0].rearrange("(t p) -> p t", p=P),
                         allow_slow_non_contiguous=True).then_inc(small_in, 16)
            sp.dma_start(inv[:, :], rope_inv.partition_broadcast(P)).then_inc(small_in, 16)
            sp.dma_start(qk_norm[:, 0, :], nsa_q_norm[0].partition_broadcast(P)).then_inc(small_in, 16)
            sp.dma_start(qk_norm[:, 1:4, :], nsa_k_norm[0].partition_broadcast(P)).then_inc(small_in, 16)
            sp.dma_start(gla_norm[:, :], gla_out_norm[0].partition_broadcast(P)).then_inc(small_in, 16)
            sp.dma_start(walpha[:, :], w_gla_alpha[0]).then_inc(small_in, 16)
            for kind, w in enumerate((w_cmp_k2, w_cmp_v2)):
                for c in range(2):
                    sp.dma_start(w2[:, kind, :, c, :], w[0].rearrange("(b f) d -> f b d", f=P)).then_inc(small_in, 16)
            for n in range(1, len(loads)):
                if loads[n][0] == "za0" and loads[n][1] == 0:
                    sp.wait_ge(go_rstd_done.sem, go_rstd_done.of(1, 1))
                    sp.wait_ge(chunk_mult_done.sem, chunk_mult_done.of())
                    sp.wait_ge(level_diff_done.sem, level_diff_done.of("tiles"))
                    sp.wait_ge(level_k_done.sem, level_k_done.of(5))
                    sp.wait_ge(level_q_done.sem, level_q_done.of(5))
                    sp.dma_start(memx, mem[0].rearrange("(t p) n -> p t n", p=P)).then_inc(mem_in, 16)
                weights(n)
            for i in range(2):
                for t in range(NT):
                    sp.wait_ge(final_done.sem, final_done.of(i,
                            t))
                    sp.dma_start(out[0, t * P:(t + 1) * P, i * NCOL:(i + 1) * NCOL],
                                 xtok[:, t, i * NCOL:(i + 1) * NCOL]).then_inc(out_written, 16)
            sp.wait_ge(out_written, 16 * 2 * NT)

        @block.tensor
        def _(pe):
            def turn(bank, sources):
                for n, src in enumerate(sources):
                    k = src.shape[0]
                    ins = pe.transpose(bank[0:src.shape[1], n * P:n * P + k], src, ident[0:k, 0:k])
                return ins

            def piece(tick):
                job, s = TICKS[tick]
                first, last = s == 0, s == PIECES[job] - 1
                if first and JOBS.index(job) >= 2:
                    for reader, key in job_readers(JOBS[JOBS.index(job) - 2]):
                        pe.wait_ge(reader.sem, reader.of(*key))
                if job.startswith("cmp"):
                    kind = int(job[3])
                    pe.wait_ge(raw_sem(tick), raw_value(tick))
                    if first:
                        pe.wait_ge(cmp_blocks_done.sem, cmp_blocks_done.of(kind))
                    w = raw[:, load_of[tick] % RAW_SLOTS, :, :].rearrange("p a n -> p (a n)")
                    for c in range(8):
                        ins = pe.matmul(job_bank(job, 0)[0:60, 0:CHID], blocks[:, kind, 8 * s + c, :],
                                        w[:, c * CHID:(c + 1) * CHID], start=(first and c == 0),
                                        stop=(last and c == 7))
                    ins.then_inc(piece_done.sem, 1)
                    return
                n = order_of[tick]
                pe.wait_ge(hi_made.sem, hi_made.of(n))
                pe.wait_ge(lo_made(n).sem, lo_made(n).of(n))
                slot = n % SPLIT_SLOTS
                kn, width = (KB, SMALL) if job == "small" else (2, NCOL)
                hi = whi[:, slot, 0:kn * width].rearrange("p (k n) -> p k n", k=kn)
                lo = wlo[:, slot, 0:kn * width].rearrange("p (k n) -> p k n", k=kn)
                if job[0] == "z" or job[:2] in ("mk", "mv"):
                    ah, al = yth, ytl
                else:
                    ah, al = xth, xtl
                if s == 0:
                    if job == "mk0":
                        for g in range(4):
                            pe.wait_ge(mt_lo_done.sem, mt_lo_done.of(g))
                    if job == "kv0":
                        pe.wait_ge(xt_lo_done.sem, xt_lo_done.of(3))
                if (job[0] == "z" or job == "out0") and s % 2 == 0:
                    for t in range(NT):
                        pe.wait_ge(y_lo_done.sem, y_lo_done.of(job[1] if job[0] == "z" else "out", s // 2, t))
                for d in range(kn):
                    k = 2 * s + d if job != "small" else d
                    start, stop = k == 0, k == KB - 1
                    if job in CHAN:
                        for m in range(4):
                            o = job_bank(job, m // 2)[:, (m % 2) * SEQ:(m % 2 + 1) * SEQ]
                            c = slice(m * P, (m + 1) * P)
                            pe.matmul(o, hi[:, d, c], ah[:, k, :], start=start and m % 2 == 0, stop=False,
                                      skip_group_check=True)
                            pe.matmul(o, hi[:, d, c], al[:, k, :], start=False, stop=False, skip_group_check=True)
                            ins = pe.matmul(o, lo[:, d, c], ah[:, k, :], start=False, stop=stop,
                                            skip_group_check=True)
                    elif job == "small":
                        o = job_bank(job, 0)[0:SMALL, 0:SEQ]
                        pe.matmul(o, hi[:, d, :], ah[:, k, :], start=start, stop=False)
                        pe.matmul(o, hi[:, d, :], al[:, k, :], start=False, stop=False)
                        pe.matmul(o, lo[:, d, :], ah[:, k, :], start=False, stop=stop)
                        for t in range(NT):
                            o = job_bank(job, 1)[:, t * 64:t * 64 + NH * 3]
                            ts = slice(t * P, (t + 1) * P)
                            pe.matmul(o, ah[:, k, ts], hi[:, d, SMALL_LR:], start=start and t == 0, stop=False,
                                      skip_group_check=True)
                            pe.matmul(o, ah[:, k, ts], lo[:, d, SMALL_LR:], start=False, stop=False,
                                      skip_group_check=True)
                            ins = pe.matmul(o, al[:, k, ts], hi[:, d, SMALL_LR:], start=False, stop=stop,
                                            skip_group_check=True)
                    else:
                        for t in range(NT):
                            o = job_bank(job, t)
                            ts = slice(t * P, (t + 1) * P)
                            pe.matmul(o, ah[:, k, ts], hi[:, d, :], start=start, stop=False)
                            pe.matmul(o, ah[:, k, ts], lo[:, d, :], start=False, stop=False)
                            ins = pe.matmul(o, al[:, k, ts], hi[:, d, :], start=False, stop=stop)
                ins.then_inc(piece_done.sem, 1)

            def k_turn(b, t):
                pe.wait_ge(kv_finish_done.sem, kv_finish_done.of(b, t))
                pe.wait_ge(ring_reader("k_turn", b, t), ring_read("k_turn", b, t))
                turn(ring("k_turn", b, t), [kdup[:,
                        g * P:(g + 1) * P] for g in range(NKV)]).then_inc(k_turn_done.sem, 1)

            def vc_turn(t):
                pe.wait_ge(kv_rstd_done.sem, kv_rstd_done.of(0, t))
                pe.wait_ge(ring_reader("vc_turn", t), ring_read("vc_turn", t))
                turn(ring("vc_turn", t), [vdup[:, t,
                        g * P:(g + 1) * P] for g in range(NKV)]).then_inc(vc_turn_done.sem, 1)

            def q_turn(i, t):
                pe.wait_ge(q_finish_done.sem, q_finish_done.of(i, t))
                pe.wait_ge(ring_reader("q_turn", i, t), ring_read("q_turn", i, t))
                turn(ring("q_turn", i, t), [qtok[:, t,
                        i * NCOL + g * P:i * NCOL + (g + 1) * P] for g in range(4)]).then_inc(q_turn_done.sem, 1)

            def cmp_turn(kind):
                pe.wait_ge(cmp_gelu_done.sem, cmp_gelu_done.of(kind))
                pe.wait_ge(ring_reader("cmp_turn", kind), ring_read("cmp_turn", kind))
                turn(ring("cmp_turn", kind), [hid[:, kind,
                        f * P:(f + 1) * P] for f in range(2)]).then_inc(cmp_turn_done.sem, 1)

            def kc():
                pe.wait_ge(cmp_turned_done.sem, cmp_turned_done.of(0))
                pe.wait_ge(ring_reader("kc"), ring_read("kc"))
                for f in range(2):
                    ins = pe.matmul(ring("kc")[:, 0:60], w2[:, 0, f, :, :].rearrange("p c d -> p (c d)"),
                                    hid_t[:, 0, f, :], start=(f == 0), stop=(f == 1))
                ins.then_inc(kc_done.sem, 1)

            def vc():
                pe.wait_ge(vc_spread_done.sem, vc_spread_done.of())
                pe.wait_ge(ring_reader("vc"), ring_read("vc"))
                for half in range(2):
                    for f in range(2):
                        rep = hrep[:, f, half, :, :, :].rearrange("p g h n -> p (g h n)")
                        ins = pe.matmul(ring("vc")[:, half * HD:(half + 1) * HD], rep, w2[:, 1, f, 0, :],
                                        start=(f == 0 and half == 0), stop=(f == 1), skip_group_check=True)
                ins.then_inc(vc_done.sem, 1)

            def cs(t):
                pe.wait_ge(q_turned_done.sem, q_turned_done.of(1, t))
                pe.wait_ge(kc_out_done.sem, kc_out_done.of())
                pe.wait_ge(ring_reader("cs", t), ring_read("cs", t))
                bank = ring("cs", t)
                for j in range(8):
                    pe.matmul(bank[:, 32 * j:32 * j + 32], qt[:, j, t * P:(t + 1) * P],
                              kcc[:, j // 2, :, :].rearrange("p a n -> p (a n)"), start=(j == 0), stop=False,
                              skip_group_check=True)
                m = cmask[:, t:t + 1, :].broadcast_to([P, NH, NP_])
                pe.matmul(bank[:, 0:256].rearrange("p (h n) -> p h n", h=NH), ident_b[:, :], m, start=False,
                              stop=True, skip_group_check=True).then_inc(cs_done.sem, 1)

            def cs_turn(t):
                pe.wait_ge(cs_sum_done.sem, cs_sum_done.of(t))
                pe.wait_ge(ring_reader("cs_turn", t), ring_read("cs_turn", t))
                turn(ring("cs_turn", t), [csc[:, t, 8 * u:8 * u + 8,
                        :].rearrange("p h n -> p (h n)") for u in range(2)]).then_inc(cs_turn_done.sem, 1)

            def out_free(b, t, u):
                n = out_units.index((b, t, u))
                if n:
                    pe.wait_ge(o_out_done.sem, o_out_done.of(*out_units[n - 1]))

            def o(b, t, u):
                out_free(b, t, u)
                pe.wait_ge(cs_turned_done.sem, cs_turned_done.of(t))
                pe.wait_ge(vc_out_done.sem, vc_out_done.of())
                pe.matmul(ps[:, OUT_BANK, :], cpt[:, t, u, :], vbd[:, u, :, :].rearrange("p h d -> p (h d)"),
                              start=True, stop=True).then_inc(o_done.sem, 1)

            def s(b, t, u, q):
                nh, nk = (4, P) if t == 0 else (2, 2 * P)
                if (b, t, u, q) == keys_of("pe", "s")[0]:
                    for tt in range(NT):
                        pe.wait_ge(k_turned_done.sem, k_turned_done.of(1, tt))
                        pe.wait_ge(k_turned_done.sem, k_turned_done.of(2, tt))
                        pe.wait_ge(q_turned_done.sem, q_turned_done.of(1, tt))
                pe.wait_ge(ring_reader("s", b, t, u, q), ring_read("s", b, t, u, q))
                bank = ring("s", b, t, u, q)
                for i, h8 in enumerate(unit_heads(t, q)):
                    h = 8 * u + h8
                    d = slice((h % 2) * HD, (h % 2 + 1) * HD)
                    pe.matmul(bank[:, i * nk:(i + 1) * nk], qt[d, h // 2, t * P:(t + 1) * P],
                              kt[d, b - 1, h // 4, 0:nk], start=(i == 0), stop=False, skip_group_check=True)
                diag = bank.rearrange("p (h k) -> p h k", h=nh)[:, :, nk - P:nk]
                m = causal[:, :].unsqueeze(1).broadcast_to([P, nh, P])
                pe.matmul(diag, ident_b[:, :], m, start=False, stop=True,
                        skip_group_check=True).then_inc(s_done.sem, 1)

            def p_turn(b, t, u, q):
                n = s_exp_done.place[(b, t, u, q)]
                pe.wait_ge(s_exp_done.sem, s_exp_done.of(b, t, u, q))
                pe.wait_ge(ring_reader("p_turn", b, t, u, q), ring_read("p_turn", b, t, u, q))
                turn(ring("p_turn", b, t, u, q), [probs[:, n % 2,
                        c * P:(c + 1) * P] for c in range(4)]).then_inc(p_turn_done.sem, 1)

            def pv(b, t, u, q):
                nh = 4 if t == 0 else 2
                n = p_turned_done.place[(b, t, u, q)]
                pe.wait_ge(p_turned_done.sem, p_turned_done.of(b, t, u, q))
                if q == 0:
                    out_free(b, t, u)
                for i, h8 in enumerate(unit_heads(t, q)):
                    for c in range(4 // nh):
                        g = (8 * u + h8) // 4
                        ins = pe.matmul(ps[:, OUT_BANK, h8 * HD:(h8 + 1) * HD],
                                        probs_t[:, n % 2, (i * (4 // nh) + c) * P:(i * (4 // nh) + c + 1) * P],
                                        vs[:, b - 1, c, g * HD:(g + 1) * HD], start=(q == 0 and i == 0 and c == 0),
                                        stop=True, skip_group_check=True)
                ins.then_inc(pv_done.sem, 1)

            def z(i):
                pe.wait_ge(small_out_done.sem, small_out_done.of())
                pe.wait_ge(ring_reader("z", i), ring_read("z", i))
                for m in range(2):
                    h = 2 * i + m
                    ins = pe.matmul(ring("z", i)[:, m * SEQ:(m + 1) * SEQ], walpha[:, h * P:(h + 1) * P], lrt[:, :],
                                    start=(m == 0), stop=True, skip_group_check=True)
                ins.then_inc(z_done.sem, 1)

            def level(lv, t):
                if lv == "diag":
                    k, q = kg, qg
                    pe.wait_ge(gqk_out_done.sem, gqk_out_done.of("gk0"))
                elif lv == "chunk":
                    k, q = kh, qh
                    pe.wait_ge(chunk_mult_done.sem, chunk_mult_done.of())
                else:
                    n = 6 if lv == "tiles" else lv
                    k = lvk[n % 2].rearrange("p (h s) -> p h s", h=GH)
                    q = lvq[n % 2].rearrange("p (h s) -> p h s", h=GH)
                    if lv == "tiles":
                        pe.wait_ge(level_diff_done.sem, level_diff_done.of(lv))
                    else:
                        pe.wait_ge(level_k_done.sem, level_k_done.of(lv))
                        pe.wait_ge(level_q_done.sem, level_q_done.of(lv))
                pe.wait_ge(ring_reader("level", lv, t), ring_read("level", lv, t))
                tq = 1 if lv == "tiles" else t
                for h in range(GH):
                    ins = pe.matmul(ring("level", lv, t)[:, h * P:(h + 1) * P], k[:, h, t * P:(t + 1) * P],
                                    q[:, h, tq * P:(tq + 1) * P], start=(h == 0), stop=True, skip_group_check=True)
                ins.then_inc(level_done.sem, 1)

            def go(t, hp):
                pe.wait_ge(level_take_done.sem, level_take_done.of("tiles", 0))
                pe.wait_ge(gv_out_done.sem, gv_out_done.of(1, 1))
                pe.wait_ge(ring_reader("go", t, hp), ring_read("go", t, hp))
                for i in range(2):
                    h = 2 * hp + i
                    o = ring("go", t, hp)[:, i * DV:(i + 1) * DV]
                    ins = pe.matmul(o, att[:, t, h, :], vg[:, t, h * DV:(h + 1) * DV], start=(i == 0),
                                    stop=(t == 0), skip_group_check=True)
                    if t == 1:
                        ins = pe.matmul(o, att10[:, h, :], vg[:, 0, h * DV:(h + 1) * DV], start=False, stop=True,
                                        skip_group_check=True)
                ins.then_inc(go_done.sem, 1)

            def y_turn(c, i, t):
                src = {"a": oa, "b": ob, "m": ob, "out": acc}[c]
                if c == "b":
                    pe.wait_ge(nsa_gate_done.sem, nsa_gate_done.of(i, t))
                elif c == "a":
                    pe.wait_ge(go_out_done.sem, go_out_done.of(t, i))
                elif c == "m":
                    pe.wait_ge(mo_out_done.sem, mo_out_done.of(t, i))
                else:
                    pe.wait_ge(mix_add_dve.sem, mix_add_dve.of("m", i, t))
                pe.wait_ge(ring_reader("y_turn", c, i, t), ring_read("y_turn", c, i, t))
                turn(ring("y_turn", c, i, t), [src[:, t,
                        i * NCOL + g * P:i * NCOL + (g + 1) * P] for g in range(4)]).then_inc(y_turn_done.sem, 1)

            def mt_turn(g):
                for t in range(NT):
                    pe.wait_ge(mem_norm_done.sem, mem_norm_done.of(t))
                pe.wait_ge(ring_reader("mt_turn", g), ring_read("mt_turn", g))
                turn(ring("mt_turn", g), [memx[:, t, (2 * g + k) * P:(2 * g + k + 1) * P]
                                       for k in range(2) for t in range(NT)]).then_inc(mt_turn_done.sem, 1)

            def mq_sum(i):
                pe.wait_ge(mq_square_done.sem, mq_square_done.of(i))
                pe.wait_ge(ring_reader("mq_sum", i), ring_read("mq_sum", i))
                for m in range(2):
                    for t in range(NT):
                        for c in range(2):
                            ins = pe.matmul(ring("mq_sum", i)[:, m * NT + t:m * NT + t + 1],
                                            msq[:, 2 * 0 + m, c * SEQ + t * P:c * SEQ + (t + 1) * P], ones[:, 0:1],
                                            start=(m == 0 and t == 0 and c == 0), stop=(c == 1),
                                            skip_group_check=True)
                ins.then_inc(mq_sum_done.sem, 1)

            def mk_sum(i):
                pe.wait_ge(mk_square_done.sem, mk_square_done.of(i))
                pe.wait_ge(ring_reader("mk_sum", i), ring_read("mk_sum", i))
                for m in range(2):
                    for c in range(2):
                        ins = pe.matmul(ring("mk_sum", i)[:, m * SEQ:(m + 1) * SEQ], ones[:, :],
                                        msq[:, 2 + m, c * SEQ:(c + 1) * SEQ], start=(m == 0 and c == 0),
                                        stop=(c == 1), skip_group_check=True)
                ins.then_inc(mk_sum_done.sem, 1)

            def ms(t, hp):
                pe.wait_ge(mk_norm_done.sem, mk_norm_done.of(1))
                pe.wait_ge(mq_rstd_done.sem, mq_rstd_done.of(1))
                pe.wait_ge(ring_reader("ms", t, hp), ring_read("ms", t, hp))
                for i in range(2):
                    for c in range(2):
                        ins = pe.matmul(ring("ms", t, hp)[:, i * MEM:(i + 1) * MEM],
                                        mqt[:, 2 * hp + i, c, t * P:(t + 1) * P], mkt[:, 2 * hp + i, c, :],
                                        start=(i == 0 and c == 0), stop=(c == 1), skip_group_check=True)
                ins.then_inc(ms_done.sem, 1)

            def mp_turn(t, hp):
                pe.wait_ge(ms_exp_done.sem, ms_exp_done.of(t, hp))
                n = ms_exp_done.place[(t, hp)]
                pe.wait_ge(ring_reader("mp_turn", t, hp), ring_read("mp_turn", t, hp))
                turn(ring("mp_turn", t, hp), [mprobs[:, n % 2,
                        c * P:(c + 1) * P] for c in range(4)]).then_inc(mp_turn_done.sem, 1)

            def mo(t, hp):
                pe.wait_ge(mp_turned_done.sem, mp_turned_done.of(t, hp))
                n = mp_turned_done.place[(t, hp)]
                pe.wait_ge(ring_reader("mo", t, hp), ring_read("mo", t, hp))
                for i in range(2):
                    for c in range(2):
                        ins = pe.matmul(ring("mo", t, hp)[:, i * MHD:(i + 1) * MHD],
                                        mprobs_t[:, n % 2, (2 * i + c) * P:(2 * i + c + 1) * P],
                                        mv[:, c, (2 * hp + i) * MHD:(2 * hp + i + 1) * MHD],
                                        start=(i == 0 and c == 0), stop=(c == 1), skip_group_check=True)
                ins.then_inc(mo_done.sem, 1)

            steps = {f.__name__: f for f in (k_turn, vc_turn, q_turn, cmp_turn, kc, vc, cs, cs_turn, o, s, p_turn, pv,
                                             z, level, go, y_turn, mt_turn, mq_sum, mk_sum, ms, mp_turn, mo)}
            pe.wait_ge(consts, 1)
            pe.wait_ge(vec_in, 16 * 7)
            turn(ring("vec_turn"), [vec[:, :]]).then_inc(vec_turn_done.sem, 1)
            for g in range(4):
                pe.wait_ge(x_norm_done.sem, x_norm_done.of(1))
                if g >= len(RING_BANKS) - 1:
                    pe.wait_ge(ring_reader("xt_turn", g), ring_read("xt_turn", g))
                turn(ring("xt_turn", g), [ob[:, t, (2 * g + k) * P:(2 * g + k + 1) * P]
                                       for k in range(2) for t in range(NT)]).then_inc(xt_turn_done.sem, 1)
            pe.wait_ge(consts, 2)
            for tick in range(len(PLAN["pe"])):
                if tick < NTICK:
                    piece(tick)
                for name, key in PLAN["pe"][tick]:
                    steps[name](*key)

        def job_pair(job):
            b0 = (JOBS.index(job) % 2) * 2
            return ps[:, b0:b0 + 2, :]

        @block.scalar
        def _(act):
            act_links = Count()
            loaded = [None]

            def f(out_, in_, func, **kw):
                if TABLE_SET.get(func, loaded[0]) != loaded[0]:
                    loaded[0] = TABLE_SET[func]
                    act.preload_act_table_set(loaded[0])
                return act.activation(out_, in_, func, **kw)

            def hi_half(tick):
                n = order_of[tick]
                act.wait_ge(raw_sem(tick), raw_value(tick))
                if TICKS[tick][0] == "small":
                    act.wait_ge(small_w, 16)
                if n >= SPLIT_SLOTS:
                    act.wait_ge(piece_done.sem, piece_done.of(splits[n - SPLIT_SLOTS]))
                act.copy(whi[:, n % SPLIT_SLOTS, 0:split_width(tick)], raw_piece(tick)).then_inc(hi_made.sem, 1)

            def rsqrt(out_, in_, width, bias=None):
                f(out_, in_, ACT.Ln, bias=eps[:, :], scale=1.0 / width).then_inc(act_chain, 1)
                act.wait_ge(act_chain, act_links.next())
                return f(out_, out_, ACT.Exp, scale=-0.5, **({"bias": bias} if bias is not None else {}))

            def kv_square(b, t):
                act.wait_ge(piece_done.sem, job_end(f"kv{b}"))
                if (b, t) != (0, 0):
                    act.wait_ge(kv_sum_done.sem, kv_sum_done.of(*((b, 0) if t else (b - 1, 1))))
                bank = job_bank(f"kv{b}", t)
                f(squares[:, 0:256], bank[:, 0:256], ACT.Square)
                v = bank[:, 256:512]
                if b == 0:
                    o = vdup[:, t, :].rearrange("p (g c d) -> p g c d", g=NKV, c=2)
                    v = v.rearrange("p (g d) -> p g d", g=NKV).unsqueeze(2).broadcast_to([P, NKV, 2, HD])
                    act.copy(o, v).then_inc(kv_square_done.sem, 1)
                else:
                    act.copy(vs[:, b - 1, t, :], v).then_inc(kv_square_done.sem, 1)

            def kv_rstd(b, t):
                act.wait_ge(kv_sum_done.sem, kv_sum_done.of(b, t))
                rsqrt(rsk[:, b, t, :], ssk[:, b, t, :], HD).then_inc(kv_rstd_done.sem, 1)

            def k_turned(b, t):
                act.wait_ge(k_turn_done.sem, k_turn_done.of(b, t))
                dst = ct[:, 0] if b == 0 else kt[:, b - 1]
                act.copy(dst[:, :, t * P:(t + 1) * P], ring("k_turn", b, t).rearrange("p (g s) -> p g s",
                        g=NKV)).then_inc(k_turned_done.sem, 1)

            def vc_turned(t):
                act.wait_ge(vc_turn_done.sem, vc_turn_done.of(t))
                act.copy(ct[:, 1, :, t * P:(t + 1) * P], ring("vc_turn", t).rearrange("p (g s) -> p g s",
                        g=NKV)).then_inc(vc_turned_done.sem, 1)

            def q_square(i, t):
                act.wait_ge(piece_done.sem, job_end(f"nq{i}"))
                if (i, t) == (0, 0):
                    act.wait_ge(kv_sum_done.sem, kv_sum_done.of(2, 1))
                else:
                    act.wait_ge(q_sum_done.sem, q_sum_done.of(*((i, 0) if t else (i - 1, 1))))
                f(squares, job_bank(f"nq{i}", t), ACT.Square).then_inc(q_square_done.sem, 1)

            def q_turned(i, t):
                act.wait_ge(q_turn_done.sem, q_turn_done.of(i, t))
                act.copy(qt[:, 4 * i:4 * i + 4, t * P:(t + 1) * P],
                             ring("q_turn", i, t).rearrange("p (g s) -> p g s", g=4)).then_inc(q_turned_done.sem, 1)

            def q_rstd():
                act.wait_ge(q_sum_done.sem, q_sum_done.of(1, 1))
                rsqrt(rsq[:, :, :], ssq[:, :, :], HD, bias=ln_scale[:, 0:1]).then_inc(q_rstd_done.sem, 1)

            def small_out():
                act.wait_ge(piece_done.sem, job_end("small"))
                act.copy(lrt[:, :], job_bank("small", 0)[0:RANK, 0:SEQ])
                g = job_bank("small", 1)[:, 0:128].rearrange("p (t n) -> p t n", t=NT)[:, :, 0:NH * 3]
                f(gates[:, :, :], g, ACT.Exp, scale=-1.0).then_inc(small_out_done.sem, 1)

            def cmp_gelu(kind):
                act.wait_ge(piece_done.sem, job_end(f"cmp{kind}"))
                f(hid[:, kind, :], job_bank(f"cmp{kind}", 0)[0:60, 0:CHID],
                        ACT.Gelu_apprx_tanh).then_inc(cmp_gelu_done.sem, 1)

            def cs_exp(t):
                act.wait_ge(cs_max_done.sem, cs_max_done.of(t))
                f(csc[:, t, :, :], csc[:, t, :, :], ACT.Exp).then_inc(cs_exp_done.sem, 1)

            def s_exp(b, t, u, q):
                nh, nk = (4, P) if t == 0 else (2, 2 * P)
                n = s_exp_done.place[(b, t, u, q)]
                act.wait_ge(s_max_done.sem, s_max_done.of(b, t, u, q))
                if n == 0:
                    act.wait_ge(cmp_blocks_done.sem, cmp_blocks_done.of(1))
                if n >= 2:
                    act.wait_ge(p_turn_done.sem, n - 1)
                bank = ring("s", b, t, u, q)
                for i, h8 in enumerate(unit_heads(t, q)):
                    h = 8 * u + h8
                    ins = f(probs[:, n % 2, i * nk:(i + 1) * nk], bank[:, i * nk:(i + 1) * nk], ACT.Exp,
                            bias=nbias[:, n % 4, i:i + 1], scale=rsq[:, t, h:h + 1],
                            accum_out=ssum[:, b, t, h:h + 1])
                ins.then_inc(s_exp_done.sem, 1)

            def gqk_out(job):
                act.wait_ge(piece_done.sem, job_end(job))
                dst = (qg if job == "gq0" else kg).rearrange("p h s -> p (h s)")
                src = job_pair(job).rearrange("p b n -> p (b n)")
                act.mul(dst, src, DK ** -0.5 if job == "gq0" else 1.0).then_inc(gqk_out_done.sem, 1)

            def silu(job, t):
                act.wait_ge(piece_done.sem, job_end(job))
                i = int(job[2])
                cols = slice(i * NCOL, (i + 1) * NCOL)
                if job[0] == "g":
                    act.wait_ge(piece_done.sem, piece_done.of(TICK_OF["cmp1"] + 1))
                    dst = oa[:, t, cols]
                elif job[0] == "n":
                    for b in (1, 2):
                        act.wait_ge(o_out_done.sem, o_out_done.of(b, 1, 1))
                    if i:
                        act.wait_ge(nsa_gate_done.sem, nsa_gate_done.of(0, t))
                    dst = zgate[:, t, :]
                else:
                    for ii in range(2):
                        act.wait_ge(y_turn_done.sem, y_turn_done.of("b", ii, t))
                    dst = ob[:, t, cols]
                f(dst, job_bank(job, t), ACT.Silu).then_inc(silu_done.sem, 1)

            def z_abs(i):
                act.wait_ge(z_done.sem, z_done.of(i))
                for tt in range(NT):
                    for uu in range(2):
                        act.wait_ge(o_out_done.sem, o_out_done.of(0, tt, uu))
                for m in range(2):
                    h = 2 * i + m
                    ins = f(gexp[:, h * SEQ:(h + 1) * SEQ], ring("z", i)[:, m * SEQ:(m + 1) * SEQ], ACT.Abs,
                            bias=balpha[:, h:h + 1])
                ins.then_inc(z_abs_done.sem, 1)

            def z_log():
                act.wait_ge(z_abs_done.sem, z_abs_done.of(1))
                f(gexp, gexp, ACT.Exp, scale=-1.0).then_inc(act_chain, 1)
                act.wait_ge(act_chain, act_links.next())
                f(gexp, gexp, ACT.Ln, bias=1.0).then_inc(z_log_done.sem, 1)

            def chunk_exp_q():
                act.wait_ge(cumsum_done.sem, cumsum_done.of())
                f(gexp, gsum, ACT.Exp, scale=1.0 / TAU).then_inc(act_chain, 1)
                act.wait_ge(act_chain, act_links.next())
                last = gsum.rearrange("p (h c s) -> p h c s", h=GH, c=4)[:, :, :, CHUNK - 1]
                f(glast[:, :, :], last, ACT.Exp, scale=1.0 / TAU).then_inc(chunk_exp_q_done.sem, 1)

            def chunk_exp_k():
                act.wait_ge(chunk_k_done.sem, chunk_k_done.of())
                f(lvk[0], lvk[0], ACT.Exp, scale=1.0 / TAU).then_inc(chunk_exp_k_done.sem, 1)

            def level_exp(lv):
                act.wait_ge(level_diff_done.sem, level_diff_done.of(lv))
                f(gexp, gexp, ACT.Exp, scale=1.0 / TAU).then_inc(level_exp_done.sem, 1)

            def go_rstd(t, hp):
                act.wait_ge(go_done.sem, go_done.of(t, hp))
                act.wait_ge(level_q_done.sem, level_q_done.of(5))
                act.wait_ge(level_k_done.sem, level_k_done.of(5))
                for i in range(2):
                    ins = f(gexp[:, 0:DV], ring("go", t, hp)[:, i * DV:(i + 1) * DV], ACT.Square,
                            accum_out=sso[:, t, 2 * hp + i:2 * hp + i + 1])
                    ins.then_inc(act_chain, 1)
                    act.wait_ge(act_chain, act_links.next())
                rsqrt(rso[:, t, 2 * hp:2 * hp + 2], sso[:, t, 2 * hp:2 * hp + 2], DV).then_inc(go_rstd_done.sem, 1)

            def y_hi(c, i, t):
                act.wait_ge(y_turn_done.sem, y_turn_done.of(c, i, t))
                last_user = {"b": None, "a": "zb1", "m": "mv1", "out": "mgm1"}[c]
                if last_user:
                    act.wait_ge(piece_done.sem,
                            job_end(last_user))
                dst = (xth if c == "out" else yth)[:, 4 * i:4 * i + 4, t * P:(t + 1) * P]
                act.copy(dst, ring("y_turn", c, i, t).rearrange("p (g s) -> p g s", g=4)).then_inc(y_hi_done.sem, 1)

            def merge(c, i, t):
                act.wait_ge(piece_done.sem, job_end(f"mg{c}{i}"))
                if c != "b":
                    act.wait_ge(mix_done.sem, mix_done.of({"a": "b", "m": "a"}[c], i, t))
                else:
                    act.wait_ge(q_turned_done.sem, q_turned_done.of(1, 1))
                    act.wait_ge(q_finish_done.sem, q_finish_done.of(1, 1))
                f(mgate[:, i, t, :], job_bank(f"mg{c}{i}", t), ACT.Sigmoid).then_inc(merge_done.sem, 1)

            def mem_square(t):
                act.wait_ge(mem_in, 16)
                if t == 0:
                    act.wait_ge(nsa_gate_done.sem, nsa_gate_done.of(1, 1))
                f(zgate[:, :, :].rearrange("p t n -> p (t n)"), memx[:, t, :], ACT.Square,
                       accum_out=ssx[:, 2 + t:3 + t]).then_inc(act_chain, 1)
                act.wait_ge(act_chain, act_links.next())

            def mem_rstd():
                rsqrt(rsx[:, 2:4], ssx[:, 2:4], D).then_inc(mem_rstd_done.sem, 1)

            def mt_hi(g):
                act.wait_ge(mt_turn_done.sem, mt_turn_done.of(g))
                act.wait_ge(piece_done.sem, job_end("za1"))
                for k in range(2):
                    ins = f(yth[:, 2 * g + k, :], ring("mt_turn", g)[:, k * SEQ:(k + 1) * SEQ], ACT.Copy,
                            scale=mgain[:, 2 * g + k:2 * g + k + 1])
                ins.then_inc(mt_hi_done.sem, 1)

            def mq_square(i):
                act.wait_ge(piece_done.sem, job_end(f"mq{i}"))
                act.wait_ge(level_done.sem, level_done.of("tiles", 0))
                if i:
                    act.wait_ge(mq_sum_done.sem, mq_sum_done.of(i - 1))
                f(msq[:, 0:2, :], job_pair(f"mq{i}"), ACT.Square).then_inc(mq_square_done.sem, 1)

            def mq_rstd(i):
                act.wait_ge(mq_sum_done.sem, mq_sum_done.of(i))
                dst = rsmq[:, 2 * i:2 * i + 2, :].rearrange("p h t -> p (h t)")
                rsqrt(dst, ring("mq_sum", i)[:, 0:2 * NT], MHD, bias=ln_scale[:, 1:2]).then_inc(mq_rstd_done.sem, 1)

            def mk_square(i):
                act.wait_ge(piece_done.sem, job_end(f"mk{i}"))
                if i:
                    act.wait_ge(mk_sum_done.sem, mk_sum_done.of(i - 1))
                f(msq[:, 2:4, :], job_pair(f"mk{i}"), ACT.Square).then_inc(mk_square_done.sem, 1)

            def mk_rstd(i):
                act.wait_ge(mk_sum_done.sem, mk_sum_done.of(i))
                act.wait_ge(nsa_gate_done.sem, nsa_gate_done.of(1, 1))
                rsqrt(zgate[:, i, :], ring("mk_sum", i), MHD).then_inc(mk_rstd_done.sem, 1)

            def ms_exp(t, hp):
                n = ms_exp_done.place[(t, hp)]
                act.wait_ge(ms_max_done.sem, ms_max_done.of(t, hp))
                act.wait_ge(go_out_done.sem, go_out_done.of(1, 1))
                if n >= 2:
                    act.wait_ge(mp_turn_done.sem, n - 1)
                for i in range(2):
                    h = 2 * hp + i
                    ins = f(mprobs[:, n % 2, i * MEM:(i + 1) * MEM], ring("ms", t, hp)[:, i * MEM:(i + 1) * MEM],
                            ACT.Exp, bias=nbias[:, n % 4, i:i + 1], scale=rsmq[:, h, t:t + 1],
                            accum_out=msum[:, t, h:h + 1])
                ins.then_inc(ms_exp_done.sem, 1)

            steps = {g.__name__: g for g in (
                kv_square, kv_rstd, k_turned, vc_turned, q_square, q_turned, q_rstd, small_out, cmp_gelu, cs_exp,
                s_exp, gqk_out, silu, z_abs, z_log, chunk_exp_q, chunk_exp_k, level_exp, go_rstd, y_hi, merge,
                mem_square, mem_rstd, mt_hi, mq_square, mq_rstd, mk_square, mk_rstd, ms_exp)}

            loaded[0] = TABLE_SET[ACT.Exp]
            act.preload_act_table_set(loaded[0])
            act.wait_ge(consts, 2)
            for t in range(NT):
                act.wait_ge(x_in[t], 16)
                f(oa[:, t, :], xtok[:, t, :], ACT.Square, accum_out=ssx[:, t:t + 1]).then_inc(act_chain, 1)
                act.wait_ge(act_chain, act_links.next())
            rsqrt(rsx[:, 0:2], ssx[:, 0:2], D).then_inc(x_rstd_done.sem, 1)
            hi_half(0)
            act.wait_ge(vec_turned_done.sem, vec_turned_done.of())
            for g in range(4):
                act.wait_ge(xt_turn_done.sem, xt_turn_done.of(g))
                for k in range(2):
                    ins = f(xth[:, 2 * g + k, :], ring("xt_turn", g)[:, k * SEQ:(k + 1) * SEQ], ACT.Copy,
                            scale=gain[:, 2 * g + k:2 * g + k + 1])
                ins.then_inc(xt_hi_done.sem, 1)
            for tick in range(1, AHEAD):
                hi_half(tick)
            act.wait_ge(angles_done.sem, angles_done.of())
            f(sines, ang[:, 3], ACT.Sin)
            f(ang[:, 2], ang[:, 3], ACT.Abs).then_inc(act_chain, 1)
            act.wait_ge(act_chain, act_links.next())
            f(cosines, ang[:, 2], ACT.Sin, scale=-1.0, bias=half_pi[:, :]).then_inc(sincos_done.sem, 1)
            for tick in range(len(PLAN["act"])):
                if tick + AHEAD < NTICK and is_split(tick + AHEAD):
                    hi_half(tick + AHEAD)
                for name, key in PLAN["act"][tick]:
                    steps[name](*key)

        @block.vector
        def _(dve):
            dve_links = Count()
            tt, ts, stt = dve.tensor_tensor, dve.tensor_scalar, dve.scalar_tensor_tensor

            def lo_half(tick):
                n = order_of[tick]
                dve.wait_ge(hi_made.sem, hi_made.of(n))
                if n >= SPLIT_SLOTS:
                    dve.wait_ge(piece_done.sem, piece_done.of(splits[n - SPLIT_SLOTS]))
                w, slot = split_width(tick), n % SPLIT_SLOTS
                dve.tensor_tensor(wlo[:, slot, 0:w], raw_piece(tick), whi[:, slot, 0:w].bitcast(F32),
                                  ALU.subtract).then_inc(lo_made_dve.sem, 1)

            def halves(bank, n, v, t):
                w = n * HD
                x = bank[:, 0:w].rearrange("p (h a d) -> p h a d", h=n, a=2)
                ra = rope_a[:, 0:w].rearrange("p (h a d) -> p h a d", h=n, a=2)
                rb = rope_b[:, 0:w].rearrange("p (h a d) -> p h a d", h=n, a=2)
                tt(ra, x, rope_c[:, v, t, :, :].unsqueeze(1).broadcast_to([P, n, 2, HALF]), ALU.mult)
                for a in range(2):
                    ins = tt(rb[:, :, a, :], x[:, :, 1 - a, :],
                             rope_s[:, v, t, a, :].unsqueeze(1).broadcast_to([P, n, HALF]), ALU.mult)
                return ins

            def kv_rope(b, t):
                dve.wait_ge(kv_square_done.sem, kv_square_done.of(b, t))
                dve.tensor_reduce(ssk[:, b, t, :], squares[:, 0:256].rearrange("p (g d) -> p g d", g=NKV), AX,
                                      ALU.add).then_inc(kv_sum_done.sem, 1)
                if (b, t) == (0, 0):
                    dve.wait_ge(rope_tables_done.sem, rope_tables_done.of())
                else:
                    dve.wait_ge(kv_finish_done.sem, kv_finish_done.of(*((b, 0) if t else (b - 1, 1))))
                halves(job_bank(f"kv{b}", t), NKV, 1 + b, t).then_inc(kv_rope_done.sem, 1)

            def q_rope(i, t):
                dve.wait_ge(q_square_done.sem, q_square_done.of(i, t))
                dve.tensor_reduce(ssq[:, t, 8 * i:8 * i + 8], squares.rearrange("p (g d) -> p g d", g=8), AX,
                                      ALU.add).then_inc(q_sum_done.sem, 1)
                if (i, t) == (0, 0):
                    dve.wait_ge(kv_finish_done.sem, kv_finish_done.of(2, 1))
                else:
                    dve.wait_ge(q_finish_done.sem, q_finish_done.of(*((i, 0) if t else (i - 1, 1))))
                halves(job_bank(f"nq{i}", t), 8, 0, t).then_inc(q_rope_done.sem, 1)

            def gates_():
                dve.wait_ge(small_out_done.sem, small_out_done.of())
                ts(gates[:, :, :], gates[:, :, :], 1.0, None, ALU.add).then_inc(dve_chain, 1)
                dve.wait_ge(dve_chain, dve_links.next())
                dve.reciprocal(gates[:, :, :], gates[:, :, :]).then_inc(gates_done.sem, 1)

            def cmp_turned(kind):
                dve.wait_ge(cmp_turn_done.sem, cmp_turn_done.of(kind))
                src = ring("cmp_turn", kind)[:, 0:256].rearrange("p (f n) -> p f n", f=2)[:, :, 0:60]
                dve.tensor_copy(hid_t[:, kind, :, :], src).then_inc(cmp_turned_done.sem, 1)

            def kc_out():
                dve.wait_ge(kc_done.sem, kc_done.of())
                for a in range(2):
                    d = slice(a * HD, (a + 1) * HD)
                    src = ring("kc")[d, 0:60].rearrange("p (g n) -> p g n", g=NKV)
                    ins = dve.tensor_copy(kcc[d, :, a, 0:NCMP], src)
                ins.then_inc(kc_out_done.sem, 1)

            def vc_out():
                dve.wait_ge(vc_done.sem, vc_done.of())
                for u in range(2):
                    ins = tt(vbd[:, u, :, :], ring("vc")[:, u * HD:(u + 1) * HD].unsqueeze(1).broadcast_to([P, 8, HD]),
                             headsel[:, :].unsqueeze(2).broadcast_to([P, 8, HD]), ALU.mult)
                ins.then_inc(vc_out_done.sem, 1)

            def cs_max(t):
                dve.wait_ge(cs_done.sem, cs_done.of(t))
                dve.wait_ge(q_rstd_done.sem, q_rstd_done.of())
                src = ring("cs", t)[:, 0:256].rearrange("p (h n) -> p h n", h=NH)
                tt(csc[:, t, :, :], src, rsq[:, t, :].unsqueeze(2).broadcast_to([P, NH, NP_]),
                        ALU.mult).then_inc(dve_chain, 1)
                dve.wait_ge(dve_chain, dve_links.next())
                dve.tensor_reduce(csm[:, t, :], csc[:, t, :, :], AX, ALU.max).then_inc(dve_chain, 1)
                dve.wait_ge(dve_chain, dve_links.next())
                tt(csc[:, t, :, :], csc[:, t, :, :], csm[:, t, :].unsqueeze(2).broadcast_to([P, NH, NP_]),
                       ALU.subtract).then_inc(cs_max_done.sem, 1)

            def cs_sum(t):
                dve.wait_ge(cs_exp_done.sem, cs_exp_done.of(t))
                dve.tensor_reduce(csm[:, t, :], csc[:, t, :, :], AX, ALU.add).then_inc(dve_chain, 1)
                dve.wait_ge(dve_chain, dve_links.next())
                tt(csc[:, t, :, :], csc[:, t, :, :], cvalid[:, t, :].unsqueeze(1).broadcast_to([P, NH, NP_]),
                       ALU.mult).then_inc(cs_sum_done.sem, 1)

            def cs_turned(t):
                dve.wait_ge(cs_turn_done.sem, cs_turn_done.of(t))
                dve.tensor_copy(cpt[:, t, :, :], ring("cs_turn", t)[:, 0:256].rearrange("p (u q) -> p u q",
                        u=2)).then_inc(cs_turned_done.sem, 1)

            def s_max(b, t, u, q):
                nh, nk = (4, P) if t == 0 else (2, 2 * P)
                n = s_max_done.place[(b, t, u, q)]
                dve.wait_ge(s_done.sem, s_done.of(b, t, u, q))
                if n >= 4:
                    dve.wait_ge(s_exp_done.sem, n - 3)
                dve.tensor_reduce(smax[:, n % 4, 0:nh], ring("s", b, t, u, q).rearrange("p (h k) -> p h k", h=nh),
                                       AX, ALU.max).then_inc(dve_chain, 1)
                dve.wait_ge(dve_chain, dve_links.next())
                h = unit_heads(t, q)
                hs = slice(8 * u + h[0], 8 * u + h[-1] + 1, 2)
                stt(nbias[:, n % 4, 0:nh], smax[:, n % 4, 0:nh], -1.0, rsq[:, t, hs], ALU.mult,
                        ALU.mult).then_inc(s_max_done.sem, 1)

            def p_turned(b, t, u, q):
                n = p_turned_done.place[(b, t, u, q)]
                dve.wait_ge(p_turn_done.sem, p_turn_done.of(b, t, u, q))
                if n >= 2:
                    dve.wait_ge(pv_done.sem, n - 1)
                dve.tensor_copy(probs_t[:, n % 2, :], ring("p_turn", b, t, u, q)).then_inc(p_turned_done.sem, 1)

            def o_out(b, t, u):
                hs = slice(8 * u, 8 * u + 8)
                dve.wait_ge(gates_done.sem, gates_done.of())
                if b == 0:
                    dve.wait_ge(o_done.sem, o_done.of(b, t, u))
                    sums = csm[:, t, hs]
                else:
                    dve.wait_ge(pv_done.sem, pv_done.of(b, t, u, 1 if t == 0 else 3))
                    sums = ssum[:, b, t, hs]
                dve.reciprocal(oweight[:, :], sums).then_inc(dve_chain, 1)
                dve.wait_ge(dve_chain, dve_links.next())
                g = gates[:, t, :].rearrange("p (h b) -> p h b", b=3)[:, hs, b]
                tt(oweight[:, :], oweight[:, :], g, ALU.mult).then_inc(dve_chain, 1)
                dve.wait_ge(dve_chain, dve_links.next())
                w = oweight[:, :].unsqueeze(2).broadcast_to([P, 8, HD])
                src = ps[:, OUT_BANK, :].rearrange("p (h d) -> p h d", h=8)
                dst = ob[:, t, u * NCOL:(u + 1) * NCOL]
                if b == 0:
                    tt(dst.rearrange("p (h d) -> p h d", h=8), src, w, ALU.mult).then_inc(o_out_done.sem, 1)
                else:
                    tt(oprod.rearrange("p (h d) -> p h d", h=8), src, w, ALU.mult).then_inc(dve_chain, 1)
                    dve.wait_ge(dve_chain, dve_links.next())
                    tt(dst, dst, oprod, ALU.add).then_inc(o_out_done.sem, 1)

            def gv_out(i, t):
                dve.wait_ge(piece_done.sem, job_end(f"gv{i}"))
                dve.tensor_copy(vg[:, t, i * NCOL:(i + 1) * NCOL], job_bank(f"gv{i}", t)).then_inc(gv_out_done.sem, 1)

            def z_min(i):
                dve.wait_ge(z_abs_done.sem, z_abs_done.of(i))
                dve.wait_ge(vc_turn_done.sem,
                        vc_turn_done.of(1))
                dve.wait_ge(vc_done.sem, vc_done.of())
                for m in range(2):
                    h = 2 * i + m
                    ins = ts(lvk[0][:, h * SEQ:(h + 1) * SEQ], ring("z", i)[:, m * SEQ:(m + 1) * SEQ],
                             balpha[:, h:h + 1], 0.0, ALU.add, ALU.min)
                ins.then_inc(z_min_done.sem, 1)

            def cumsum():
                dve.wait_ge(z_log_done.sem, z_log_done.of())
                dve.wait_ge(z_min_done.sem, z_min_done.of(1))
                reset = lvq[0]
                dve.memset(reset, 1.0).then_inc(dve_chain, 1)
                dve.wait_ge(dve_chain, dve_links.next())
                dve.memset(reset.rearrange("p (c s) -> p c s", s=CHUNK)[:, :, 0:1], 0.0).then_inc(dve_chain, 1)
                dve.wait_ge(dve_chain, dve_links.next())
                tt(lvk[0], lvk[0], gexp, ALU.subtract).then_inc(dve_chain, 1)
                dve.wait_ge(dve_chain, dve_links.next())
                dve.tensor_tensor_scan(gsum, reset, lvk[0], 0.0, ALU.mult, ALU.add).then_inc(cumsum_done.sem, 1)

            def chunk_k():
                dve.wait_ge(cumsum_done.sem, cumsum_done.of())
                g = gsum.rearrange("p (c s) -> p c s", s=CHUNK)
                tt(lvk[0].rearrange("p (c s) -> p c s", s=CHUNK),
                       g[:, :, CHUNK - 1:CHUNK].broadcast_to([P, 16, CHUNK]), g, ALU.subtract).then_inc(chunk_k_done.sem, 1)

            def chunk_mult():
                last = keys_of("pe", "pv")[-1]
                dve.wait_ge(pv_done.sem, pv_done.of(*last))
                dve.wait_ge(o_out_done.sem, o_out_done.of(*out_units[-1]))
                dve.memset(s3[:, 0:1024], 0.0).then_inc(dve_chain, 1)
                dve.wait_ge(dve_chain, dve_links.next())
                dve.wait_ge(gqk_out_done.sem, gqk_out_done.of("gk0"))
                dve.wait_ge(chunk_exp_q_done.sem, chunk_exp_q_done.of())
                dve.wait_ge(chunk_exp_k_done.sem, chunk_exp_k_done.of())
                tt(kh.rearrange("p h s -> p (h s)"), kg.rearrange("p h s -> p (h s)"), lvk[0],
                        ALU.mult).then_inc(dve_chain, 1)
                dve.wait_ge(dve_chain, dve_links.next())
                tt(qh.rearrange("p h s -> p (h s)"), qg.rearrange("p h s -> p (h s)"), gexp,
                        ALU.mult).then_inc(chunk_mult_done.sem, 1)

            def level_diff(lv):
                dve.wait_ge(chunk_mult_done.sem, chunk_mult_done.of())
                if lv == "tiles":
                    dve.wait_ge(level_done.sem, level_done.of(4, 1))
                    k4 = lvk[0].rearrange("p (h c s) -> p h c s", h=GH, c=4)
                    q4 = lvq[0].rearrange("p (h c s) -> p h c s", h=GH, c=4)
                    kh4 = kh.rearrange("p h (c s) -> p h c s", c=4)
                    qh4 = qh.rearrange("p h (c s) -> p h c s", c=4)
                    dve.tensor_copy(k4[:, :, 1, :], kh4[:, :, 1, :])
                    tt(k4[:, :, 0, :], kh4[:, :, 0, :], glast[:, :, 1:2].broadcast_to([P, GH, CHUNK]), ALU.mult)
                    dve.tensor_copy(q4[:, :, 2, :], qh4[:, :, 2, :])
                    tt(q4[:, :, 3, :], qh4[:, :, 3, :], glast[:, :, 2:3].broadcast_to([P, GH, CHUNK]),
                            ALU.mult).then_inc(level_diff_done.sem, 1)
                    return
                if lv > 0:
                    dve.wait_ge(level_k_done.sem, level_k_done.of(lv - 1))
                    dve.wait_ge(level_q_done.sem, level_q_done.of(lv - 1))
                half = CHUNK >> (lv + 1)
                g = gsum.rearrange("p (b a s) -> p b a s", a=2, s=half)
                d = gexp.rearrange("p (b a s) -> p b a s", a=2, s=half)
                nb = SEQ * GH // (2 * half)
                r = g[:, :, 0, half - 1:half].broadcast_to([P, nb, half])
                tt(d[:, :, 0, :], r, g[:, :, 0, :], ALU.subtract)
                tt(d[:, :, 1, :], g[:, :, 1, :], r, ALU.subtract).then_inc(level_diff_done.sem, 1)

            def level_k(lv):
                dve.wait_ge(level_exp_done.sem, level_exp_done.of(lv))
                if lv >= 2:
                    dve.wait_ge(level_done.sem, level_done.of(lv - 2, 1))
                half = CHUNK >> (lv + 1)
                v = "p (b a s) -> p b a s"
                k = kg.rearrange("p h s -> p (h s)").rearrange(v, a=2, s=half)
                tt(lvk[lv % 2].rearrange(v, a=2, s=half)[:, :, 0, :], k[:, :, 0, :],
                       gexp.rearrange(v, a=2, s=half)[:, :, 0, :], ALU.mult).then_inc(level_k_done.sem, 1)

            def level_take(lv, t):
                dve.wait_ge(level_done.sem, level_done.of(lv, t))
                n = level_take_done.place[(lv, t)]
                if n >= NT:
                    dve.wait_ge(level_take_done.sem, level_take_done.of(*keys_of("dve", "level_take")[n - NT]))
                src = ring("level", lv, t).rearrange("p (h i) -> p h i", h=GH)
                if lv == "tiles":
                    ins = dve.tensor_copy(att10, src)
                elif lv == "chunk":
                    ins = dve.tensor_copy(att[0:CHUNK, t, :, CHUNK:], src[0:CHUNK, :, CHUNK:])
                else:
                    dve.wait_ge(consts, 3)
                    m = lmask[:, 6 if lv == "diag" else lv, :].unsqueeze(1).broadcast_to([P, GH, P])
                    ins = dve.copy_predicated(att[:, t, :, :], m, src)
                ins.then_inc(level_take_done.sem, 1)

            def go_out(t, hp):
                dve.wait_ge(go_rstd_done.sem, go_rstd_done.of(t, hp))
                dve.wait_ge(gla_gain_done.sem, gla_gain_done.of(hp, t))
                for i in range(2):
                    h = 2 * hp + i
                    y = oa[:, t, h * DV:(h + 1) * DV]
                    ins = stt(y, ring("go", t, hp)[:, i * DV:(i + 1) * DV], rso[:, t, h:h + 1], y, ALU.mult, ALU.mult)
                ins.then_inc(go_out_done.sem, 1)

            def nsa_gate(i, t):
                dve.wait_ge(silu_done.sem, silu_done.of(f"ng{i}", t))
                y = ob[:, t, i * NCOL:(i + 1) * NCOL]
                tt(y, y, zgate[:, t, :], ALU.mult).then_inc(nsa_gate_done.sem, 1)

            def y_lo(c, i, t):
                dve.wait_ge(y_hi_done.sem, y_hi_done.of(c, i, t))
                hi_, lo_ = (xth, xtl) if c == "out" else (yth, ytl)
                d = (slice(None), slice(4 * i, 4 * i + 4), slice(t * P, (t + 1) * P))
                tt(lo_[d], ring("y_turn", c, i, t).rearrange("p (g s) -> p g s", g=4), hi_[d].bitcast(F32),
                       ALU.subtract).then_inc(y_lo_done.sem, 1)

            def mix(c, i, t):
                dve.wait_ge(merge_done.sem, merge_done.of(c, i, t))
                dve.wait_ge(piece_done.sem, job_end(f"z{c}{i}"))
                bank = job_bank(f"z{c}{i}", t)
                if c == "b":
                    tt(acc[:, t, i * NCOL:(i + 1) * NCOL], bank, mgate[:, i, t, :], ALU.mult).then_inc(mix_done.sem,
                            1)
                    return
                if i or c == "m":
                    prev = (c, 0, t) if i else ("a", 1, t)
                    if prev[0] == "a":
                        dve.wait_ge(mix_add_pool.sem, mix_add_pool.of(*prev))
                else:
                    dve.wait_ge(level_diff_done.sem, level_diff_done.of("tiles"))
                tt(mixed[:, t, :], bank, mgate[:, i, t, :], ALU.mult).then_inc(mix_done.sem, 1)

            def mix_add(c, i, t):
                dve.wait_ge(mix_done.sem, mix_done.of(c, i, t))
                y = acc[:, t, i * NCOL:(i + 1) * NCOL]
                tt(y, y, mixed[:, t, :], ALU.add).then_inc(mix_add_dve.sem, 1)

            def mem_norm(t):
                dve.wait_ge(mem_rstd_done.sem, mem_rstd_done.of())
                ts(memx[:, t, :], memx[:, t, :], rsx[:, 2 + t:3 + t], None, ALU.mult).then_inc(mem_norm_done.sem, 1)

            def mt_lo(g):
                dve.wait_ge(mt_hi_done.sem, mt_hi_done.of(g))
                for k in range(2):
                    ins = stt(ytl[:, 2 * g + k, :], ring("mt_turn", g)[:, k * SEQ:(k + 1) * SEQ],
                              mgain[:, 2 * g + k:2 * g + k + 1], yth[:, 2 * g + k, :].bitcast(F32), ALU.mult,
                              ALU.subtract)
                ins.then_inc(mt_lo_done.sem, 1)

            def mq_out(i):
                dve.wait_ge(mq_square_done.sem, mq_square_done.of(i))
                dve.wait_ge(level_done.sem, level_done.of("diag", 1))
                dve.wait_ge(level_q_done.sem, level_q_done.of(5))
                for c in range(2):
                    ins = ts(mqt[:, 2 * i:2 * i + 2, c, :], job_pair(f"mq{i}")[:, :, c * SEQ:(c + 1) * SEQ],
                             mqk_gain[:, c:c + 1], None, ALU.mult)
                ins.then_inc(mq_out_done.sem, 1)

            def mk_out(i):
                dve.wait_ge(mk_square_done.sem, mk_square_done.of(i))
                dve.wait_ge(level_done.sem, level_done.of(5, 1))
                dve.tensor_copy(mkt[:, 2 * i:2 * i + 2, :, :].rearrange("p h c s -> p (h c s)"),
                                    job_pair(f"mk{i}").rearrange("p b n -> p (b n)")).then_inc(mk_out_done.sem, 1)

            def mk_norm(i):
                dve.wait_ge(mk_rstd_done.sem, mk_rstd_done.of(i))
                dve.wait_ge(mk_out_done.sem, mk_out_done.of(i))
                k = mkt[:, 2 * i:2 * i + 2, :, :]
                r = zgate[:, i, :].rearrange("p (h s) -> p h s", h=2).unsqueeze(2).broadcast_to([P, 2, 2, MEM])
                tt(k, k, r, ALU.mult).then_inc(mk_norm_done.sem, 1)

            def mv_out(i, t):
                dve.wait_ge(piece_done.sem, job_end(f"mv{i}"))
                dve.wait_ge(go_done.sem, go_done.of(1, 1))
                dve.tensor_copy(mv[:, t, i * NCOL:(i + 1) * NCOL], job_bank(f"mv{i}", t)).then_inc(mv_out_done.sem, 1)

            def ms_max(t, hp):
                n = ms_max_done.place[(t, hp)]
                dve.wait_ge(ms_done.sem, ms_done.of(t, hp))
                if n == 0:
                    dve.wait_ge(s_exp_done.sem, s_exp_done.of(*keys_of("act", "s_exp")[-1]))
                dve.tensor_reduce(smax[:, n % 4, 0:2], ring("ms", t, hp).rearrange("p (h k) -> p h k", h=2), AX,
                                       ALU.max).then_inc(dve_chain, 1)
                dve.wait_ge(dve_chain, dve_links.next())
                stt(nbias[:, n % 4, 0:2], smax[:, n % 4, 0:2], -1.0, rsmq[:, 2 * hp:2 * hp + 2, t], ALU.mult,
                        ALU.mult).then_inc(ms_max_done.sem, 1)

            def mp_turned(t, hp):
                n = mp_turned_done.place[(t, hp)]
                dve.wait_ge(mp_turn_done.sem, mp_turn_done.of(t, hp))
                if n >= 2:
                    dve.wait_ge(mo_done.sem, n - 1)
                dve.tensor_copy(mprobs_t[:, n % 2, :], ring("mp_turn", t, hp)).then_inc(mp_turned_done.sem, 1)

            def mo_out(t, hp):
                dve.wait_ge(mo_done.sem, mo_done.of(t, hp))
                dve.wait_ge(silu_done.sem, silu_done.of(f"mg{hp}", t))
                dve.reciprocal(oweight[:, 0:2], msum[:, t, 2 * hp:2 * hp + 2]).then_inc(dve_chain, 1)
                dve.wait_ge(dve_chain, dve_links.next())
                for i in range(2):
                    y = ob[:, t, (2 * hp + i) * MHD:(2 * hp + i + 1) * MHD]
                    ins = stt(y, ring("mo", t, hp)[:, i * MHD:(i + 1) * MHD], oweight[:, i:i + 1], y, ALU.mult,
                              ALU.mult)
                ins.then_inc(mo_out_done.sem, 1)

            def final(i, t):
                dve.wait_ge(piece_done.sem, job_end(f"out{i}"))
                y = xtok[:, t, i * NCOL:(i + 1) * NCOL]
                tt(y, job_bank(f"out{i}", t), y, ALU.add).then_inc(final_done.sem, 1)

            steps = {g.__name__: g for g in (
                kv_rope, q_rope, cmp_turned, kc_out, vc_out, cs_max, cs_sum, cs_turned, s_max, p_turned, o_out,
                gv_out, z_min, cumsum, chunk_k, chunk_mult, level_diff, level_k, level_take, go_out, nsa_gate, y_lo,
                mix, mix_add, mem_norm, mt_lo, mq_out, mk_out, mk_norm, mv_out, ms_max, mp_turned, mo_out, final)}
            steps["gates"] = gates_

            dve.wait_ge(vec_turn_done.sem, vec_turn_done.of())
            dve.tensor_copy(vect[:, :], ring("vec_turn")[:, 0:56]).then_inc(dve_chain, 1)
            dve.wait_ge(dve_chain, dve_links.next())
            tt(mqk_gain[:, :], vect[:, 20:22], vect[:, 22:24], ALU.mult).then_inc(vec_turned_done.sem, 1)
            dve.wait_ge(x_rstd_done.sem, x_rstd_done.of())
            for t in range(NT):
                ts(ob[:, t, :], xtok[:, t, :], rsx[:, t:t + 1], None, ALU.mult).then_inc(x_norm_done.sem, 1)
            for g in range(4):
                dve.wait_ge(xt_hi_done.sem, xt_hi_done.of(g))
                for k in range(2):
                    ins = stt(xtl[:, 2 * g + k, :], ring("xt_turn", g)[:, k * SEQ:(k + 1) * SEQ],
                              gain[:, 2 * g + k:2 * g + k + 1], xth[:, 2 * g + k, :].bitcast(F32), ALU.mult,
                              ALU.subtract)
                ins.then_inc(xt_lo_done.sem, 1)
            lo_half(0)
            lo_half(1)
            dve.wait_ge(small_in, 16 * 10)
            dve.tensor_copy(ang[:, 3, :, 0:1], pos_i[:, :].unsqueeze(2)).then_inc(dve_chain, 1)
            dve.wait_ge(dve_chain, dve_links.next())
            dve.tensor_copy(ang[:, 2, :, 0:1], ang[:, 3, :, 0:1]).then_inc(dve_chain, 1)
            dve.wait_ge(dve_chain, dve_links.next())
            for t in range(NT):
                ts(ang[:, 0, t, :], inv[:, :], ang[:, 2, t, 0:1], None, ALU.mult).then_inc(dve_chain, 1)
                dve.wait_ge(dve_chain, dve_links.next())
            ts(ang[:, 1], ang[:, 0], 1.0 / TWO_PI, MAGIC, ALU.mult, ALU.add).then_inc(dve_chain, 1)
            dve.wait_ge(dve_chain, dve_links.next())
            ts(ang[:, 1], ang[:, 1], MAGIC, None, ALU.subtract).then_inc(dve_chain, 1)
            dve.wait_ge(dve_chain, dve_links.next())
            stt(ang[:, 2], ang[:, 1], -C1, ang[:, 0], ALU.mult, ALU.add).then_inc(dve_chain, 1)
            dve.wait_ge(dve_chain, dve_links.next())
            stt(ang[:, 0], ang[:, 1], -C2, ang[:, 2], ALU.mult, ALU.add).then_inc(dve_chain, 1)
            dve.wait_ge(dve_chain, dve_links.next())
            stt(ang[:, 3], ang[:, 1], -C3, ang[:, 0], ALU.mult, ALU.add).then_inc(angles_done.sem, 1)
            for tick in range(len(PLAN["dve"])):
                if tick + AHEAD < NTICK and is_split(tick + AHEAD) and not lo_on_pool(order_of[tick + AHEAD]):
                    lo_half(tick + AHEAD)
                for name, key in PLAN["dve"][tick]:
                    steps[name](*key)

        @block.gpsimd
        def _(pool):
            pool_links = Count()
            tt = pool.tensor_tensor

            def lo_half(tick):
                n = order_of[tick]
                pool.wait_ge(hi_made.sem, hi_made.of(n))
                if n >= SPLIT_SLOTS:
                    pool.wait_ge(piece_done.sem, piece_done.of(splits[n - SPLIT_SLOTS]))
                w, slot = split_width(tick), n % SPLIT_SLOTS
                pool.tensor_tensor(wlo[:, slot, 0:w], raw_piece(tick), whi[:, slot, 0:w].bitcast(F32),
                                  ALU.subtract).then_inc(lo_made_pool.sem, 1)
                pool.wait_ge(lo_made_pool.sem, lo_made_pool.of(order_of[tick]))

            def kv_finish(b, t):
                pool.wait_ge(kv_rope_done.sem, kv_rope_done.of(b, t))
                tt(rope_a[:, 0:256], rope_a[:, 0:256], rope_b[:, 0:256], ALU.add).then_inc(pool_chain, 1)
                pool.wait_ge(pool_chain, pool_links.next())
                pool.wait_ge(kv_rstd_done.sem, kv_rstd_done.of(b, t))
                if (b, t) != (0, 0):
                    pool.wait_ge(k_turn_done.sem, k_turn_done.of(*((b, 0) if t else (b - 1, 1))))
                src = rope_a[:, 0:256].rearrange("p (g d) -> p g d", g=NKV).unsqueeze(2).broadcast_to([P, NKV, 2, HD])
                r = rsk[:, b, t, :].unsqueeze(2).unsqueeze(3).broadcast_to([P, NKV, 2, HD])
                tt(kdup.rearrange("p (g c d) -> p g c d", g=NKV, c=2), src, r,
                        ALU.mult).then_inc(kv_finish_done.sem, 1)
                pool.wait_ge(kv_finish_done.sem, kv_finish_done.of(b, t))

            def q_finish(i, t):
                pool.wait_ge(q_rope_done.sem, q_rope_done.of(i, t))
                tt(qtok[:, t, i * NCOL:(i + 1) * NCOL], rope_a, rope_b, ALU.add).then_inc(q_finish_done.sem, 1)
                pool.wait_ge(q_finish_done.sem, q_finish_done.of(i, t))

            def cmp_blocks(kind):
                if kind == 0:
                    pool.wait_ge(k_turned_done.sem, k_turned_done.of(0, 1))
                else:
                    pool.wait_ge(vc_turned_done.sem, vc_turned_done.of(1))
                for l in range(2):
                    d = slice(l * HD, (l + 1) * HD)
                    tokens = ct[d, kind].rearrange("p g (b o) -> p g b o", o=CSTRIDE)
                    for c1 in range(2):
                        src = tokens[:, :, c1:c1 + NCMP, l::2]
                        pe_ = vect[d, 24 + 16 * kind + 8 * c1:32 + 16 * kind + 8 * c1]
                        pe_ = pe_.unsqueeze(1).unsqueeze(1).broadcast_to([HD, NKV, NCMP, 8])
                        dst = blocks[d, kind, 8 * c1:8 * c1 + 8, :].rearrange("p c (g n) -> p g n c", g=NKV)
                        ins = tt(dst, src, pe_, ALU.add)
                        ins.then_inc(cmp_blocks_done.sem, 1)
                        pool.wait_ge(cmp_blocks_done.sem, cmp_blocks_done.of(kind, part=2 * l + c1))

            def vc_spread():
                pool.wait_ge(cmp_turned_done.sem, cmp_turned_done.of(1))
                for f in range(2):
                    for u in range(2):
                        src = hid_t[:, 1, f, :].rearrange("p (g n) -> p g n", g=NKV)[:, 2 * u:2 * u + 2, :]
                        ins = pool.tensor_copy(hrep[:, f, u, :, :, 0:NCMP],
                                               src.unsqueeze(2).broadcast_to([P, 2, 4, NCMP]))
                        ins.then_inc(vc_spread_done.sem, 1)
                        pool.wait_ge(vc_spread_done.sem, vc_spread_done.of(part=2 * f + u))

            def gla_gain(i, t):
                pool.wait_ge(silu_done.sem, silu_done.of(f"gg{i}", t))
                y = oa[:, t, i * NCOL:(i + 1) * NCOL].rearrange("p (h d) -> p h d", h=2)
                tt(y, y, gla_norm[:, :].unsqueeze(1).broadcast_to([P, 2, DV]), ALU.mult).then_inc(gla_gain_done.sem,
                        1)
                pool.wait_ge(gla_gain_done.sem, gla_gain_done.of(i, t))

            def level_q(lv):
                pool.wait_ge(level_exp_done.sem, level_exp_done.of(lv))
                pool.wait_ge(gqk_out_done.sem, gqk_out_done.of("gk0"))
                if lv >= 2:
                    pool.wait_ge(level_done.sem, level_done.of(lv - 2, 1))
                else:
                    pool.wait_ge(chunk_mult_done.sem, chunk_mult_done.of())
                half = CHUNK >> (lv + 1)
                v = "p (b a s) -> p b a s"
                q = qg.rearrange("p h s -> p (h s)").rearrange(v, a=2, s=half)
                tt(lvq[lv % 2].rearrange(v, a=2, s=half)[:, :, 1, :], q[:, :, 1, :],
                          gexp.rearrange(v, a=2, s=half)[:, :, 1, :], ALU.mult).then_inc(level_q_done.sem, 1)
                pool.wait_ge(level_q_done.sem, level_q_done.of(lv))

            def mix_add(c, i, t):
                pool.wait_ge(mix_done.sem, mix_done.of(c, i, t))
                y = acc[:, t, i * NCOL:(i + 1) * NCOL]
                tt(y, y, mixed[:, t, :], ALU.add).then_inc(mix_add_pool.sem, 1)
                pool.wait_ge(mix_add_pool.sem, mix_add_pool.of(c, i, t))

            def level_mask(lv):
                if lv == 6:
                    pool.tensor_copy(lmask[:, 6, :], ident[:, :]).then_inc(consts, 1)
                    pool.wait_ge(consts, 3)
                    return
                half = CHUNK >> (lv + 1)
                v = lmask_f[:, :].rearrange("p (b a s) -> p b a s", a=2, s=half) if half > 1 else \
                    lmask_f[:, :].rearrange("p (b a) -> p b a", a=2)
                inner = [[0, half]] if half > 1 else []
                nb = P // (2 * half)
                pool.memset(lmask_f[:, :], 1.0).then_inc(pool_chain, 1)
                pool.wait_ge(pool_chain, pool_links.next())
                select(v, [[-2 * half, nb], [0, 2]] + inner, 0, 1, 0.0).then_inc(pool_chain, 1)
                pool.wait_ge(pool_chain, pool_links.next())
                select(v, [[2 * half, nb], [0, 2]] + inner, half - 1, -1, 0.0).then_inc(pool_chain, 1)
                pool.wait_ge(pool_chain, pool_links.next())
                select(v, [[0, nb], [1, 2]] + inner, -1, 0, 0.0).then_inc(pool_chain, 1)
                pool.wait_ge(pool_chain, pool_links.next())
                pool.tensor_copy(lmask[:, lv, :], lmask_f[:, :]).then_inc(pool_chain, 1)
                pool.wait_ge(pool_chain, pool_links.next())

            steps = {g.__name__: g for g in (level_mask, kv_finish, q_finish, cmp_blocks, vc_spread, gla_gain, level_q, mix_add)}

            def select(tile, pattern, base, mult, fill, op=ALU.is_ge):
                return pool.affine_select(out=tile, in_=tile, pattern=pattern, compare_op=op, fill=fill, base=base,
                                          channel_multiplier=mult)

            def part(ins, n):
                ins.then_inc(consts, 1)
                pool.wait_ge(consts, n)

            pool.memset(ident[:, :], 0.0).then_inc(pool_chain, 1)
            pool.wait_ge(pool_chain, pool_links.next())
            part(select(ident[:, :], [[-1, P]], 0, 1, 1.0, ALU.not_equal), 1)
            pool.memset(eps[:, :], EPS).then_inc(pool_chain, 1)
            pool.wait_ge(pool_chain, pool_links.next())
            pool.memset(half_pi[:, :], float(np.pi / 2)).then_inc(pool_chain, 1)
            pool.wait_ge(pool_chain, pool_links.next())
            pool.memset(ln_scale[:, 0:1], float(np.log(HD ** -0.5))).then_inc(pool_chain, 1)
            pool.wait_ge(pool_chain, pool_links.next())
            pool.memset(ln_scale[:, 1:2], float(np.log(MHD ** -0.5))).then_inc(pool_chain, 1)
            pool.wait_ge(pool_chain, pool_links.next())
            pool.memset(ones[:, :], 1.0).then_inc(pool_chain, 1)
            pool.wait_ge(pool_chain, pool_links.next())
            pool.tensor_copy(ident_b[:, :], ident[:, :]).then_inc(pool_chain, 1)
            pool.wait_ge(pool_chain, pool_links.next())
            pool.memset(causal[:, :], 0.0).then_inc(pool_chain, 1)
            pool.wait_ge(pool_chain, pool_links.next())
            select(causal[:, :], [[-1, P]], 0, 1, NEG).then_inc(pool_chain, 1)
            pool.wait_ge(pool_chain, pool_links.next())
            for mask, inside, outside in ((cmask, 0.0, NEG), (cvalid, 1.0, 0.0)):
                pool.memset(mask[:, :, :], inside).then_inc(pool_chain, 1)
                pool.wait_ge(pool_chain, pool_links.next())
                select(mask[:, :, :], [[P, NT], [-CSTRIDE, NP_]], 1 - CLEN, 1, outside).then_inc(pool_chain, 1)
                pool.wait_ge(pool_chain, pool_links.next())
            pool.memset(headsel[:, :], 1.0).then_inc(pool_chain, 1)
            pool.wait_ge(pool_chain, pool_links.next())
            select(headsel[:, :], [[-NP_, 8]], 0, 1, 0.0).then_inc(pool_chain, 1)
            pool.wait_ge(pool_chain, pool_links.next())
            select(headsel[:, :], [[NP_, 8]], NP_ - 1, -1, 0.0).then_inc(pool_chain, 1)
            pool.wait_ge(pool_chain, pool_links.next())
            pool.memset(kcc[:, :, :, :], 0.0).then_inc(pool_chain, 1)
            pool.wait_ge(pool_chain, pool_links.next())
            part(pool.memset(hrep, 0.0), 2)
            pool.wait_ge(small_in, 16 * 10)
            pool.wait_ge(sincos_done.sem, sincos_done.of())
            for v in range(4):
                g = qk_norm[:, v, :].rearrange("p (a d) -> p a d", a=2)
                for a in range(2):
                    tt(rope_c[:, v, :, a, :], cosines, g[:, a:a + 1, :].broadcast_to([P, NT, HALF]),
                            ALU.mult).then_inc(pool_chain, 1)
                    pool.wait_ge(pool_chain, pool_links.next())
                    tt(rope_s[:, v, :, a, :], sines, g[:, 1 - a:2 - a, :].broadcast_to([P, NT, HALF]),
                            ALU.mult).then_inc(pool_chain, 1)
                    pool.wait_ge(pool_chain, pool_links.next())
            pool.tensor_scalar(rope_s[:, :, :, 0, :], rope_s[:, :, :, 0, :], -1.0, None,
                    ALU.mult).then_inc(rope_tables_done.sem, 1)
            pool.wait_ge(rope_tables_done.sem, rope_tables_done.of())

            for tick in range(-AHEAD, len(PLAN["pool"])):
                if tick + AHEAD < NTICK and is_split(tick + AHEAD) and lo_on_pool(order_of[tick + AHEAD]):
                    lo_half(tick + AHEAD)
                for name, key in PLAN["pool"][tick] if tick >= 0 else []:
                    steps[name](*key)


_INS = ["x", "mem", "positions", "norm_gain", "mem_norm_gain", "w_in", "w_gla_alpha", "b_gla_alpha", "gla_out_norm",
        "nsa_q_norm", "nsa_k_norm", "pe_cmp_k", "pe_cmp_v", "w_cmp_k1", "w_cmp_k2", "w_cmp_v1", "w_cmp_v2",
        "w_mem_kv", "mem_q_norm", "mem_k_norm", "w_branch", "w_out"]


def kernel(**inputs):
    import concourse.bacc as bacc
    from concourse.bass_utils import run_bass_kernel_spmd

    nc = bacc.Bacc("TRN2", target_bir_lowering=False, num_devices=1)
    arrays = {name: np.ascontiguousarray(inputs[name]) for name in _INS}
    arrays["rope_inv"] = np.float32(10000.0) ** (-np.arange(HALF, dtype=np.float32) / np.float32(HALF))
    feed, args = {}, []
    for name, a in arrays.items():
        feed[f"in_{name}"] = a
        args.append(nc.dram_tensor(f"in_{name}", a.shape, mybir.dt.from_np(a.dtype), kind="ExternalInput").ap())
    args.append(nc.dram_tensor("out_0", (1, SEQ, D), F32, kind="ExternalOutput").ap())
    layer(nc, *args)
    r = run_bass_kernel_spmd(nc, [feed], core_ids=[0])
    return r.results[0]["out_0"]
```
